# Optimizing a Trainium2 kernel written in Bass

```python
import jax, jax.numpy as jnp
from jax import lax
import numpy as np

D_MODEL = 1024
BATCH = 1
SEQ = 4096
DEPTH = 2

GRID_W = 64
CTX_LEN = 256
HEAD_DIM = 64
ATTN_DIM = D_MODEL // 2
N_Q_HEADS = ATTN_DIM // HEAD_DIM
N_KV_HEADS = N_Q_HEADS // 4
Q_PER_KV = N_Q_HEADS // N_KV_HEADS
KV_DIM = N_KV_HEADS * HEAD_DIM
WINDOW = 128
BLOCK = 128
ROPE_THETA = 10000.0
ROPE_AXIS_PAIRS = HEAD_DIM // 4
POOL_WINDOWS = (2, 4, 8, 16)
POOL_DIM = D_MODEL - ATTN_DIM
POOL_GROUP_DIM = POOL_DIM // len(POOL_WINDOWS)
AP_GATE_DIM = ATTN_DIM + POOL_DIM
AP_IN_DIM = ATTN_DIM + 2 * KV_DIM + POOL_DIM + AP_GATE_DIM
CONV_DIM = D_MODEL
CONV_K = 31
CV_IN_DIM = 3 * CONV_DIM
N_AP_LAYERS = (DEPTH + 1) // 2
N_CV_LAYERS = DEPTH // 2
EPS = 1e-6
NEG_INF = -1e30

kernel_name = "hybrid_window_gqa_pool_conformer_dit"

def _rmsnorm(x, g):
    xf = x.astype(jnp.float32)
    y = xf * lax.rsqrt(jnp.mean(xf * xf, axis=-1, keepdims=True) + EPS)
    return (y * g.astype(jnp.float32)).astype(x.dtype)

def _layernorm(x, g, b):
    xf = x.astype(jnp.float32)
    mu = jnp.mean(xf, axis=-1, keepdims=True)
    xc = xf - mu
    y = xc * lax.rsqrt(jnp.mean(xc * xc, axis=-1, keepdims=True) + EPS)
    return (y * g.astype(jnp.float32) + b.astype(jnp.float32)).astype(x.dtype)

def _modulate(x, cond, ada_w, ada_b, norm_g):
    shift, scale, gate = jnp.split(jax.nn.silu(cond) @ ada_w + ada_b, 3, axis=-1)
    h = _rmsnorm(x, norm_g) * (1 + scale) + shift
    return h, gate

def _axial_rope_tables(n_tokens):
    rows = n_tokens // GRID_W
    row = jnp.repeat(jnp.arange(rows, dtype=jnp.float32), GRID_W)
    col = jnp.tile(jnp.arange(GRID_W, dtype=jnp.float32), rows)
    inv_freq = ROPE_THETA ** (-jnp.arange(ROPE_AXIS_PAIRS, dtype=jnp.float32) / ROPE_AXIS_PAIRS)
    ang = jnp.concatenate([row[:, None] * inv_freq, col[:, None] * inv_freq], axis=-1)
    return jnp.cos(ang), jnp.sin(ang)

def _rope(x, cos, sin):
    x1, x2 = jnp.split(x.astype(jnp.float32), 2, axis=-1)
    cs, sn = cos[:, None, :], sin[:, None, :]
    return jnp.concatenate([x1 * cs - x2 * sn, x1 * sn + x2 * cs], axis=-1).astype(x.dtype)

def _heads(t, n_heads):
    return t.reshape(t.shape[:2] + (n_heads, HEAD_DIM))

def _sink_attention(q, k, v, sink, mask=None):
    s = jnp.einsum('bqhgd,bkhd->bhgqk', q, k, preferred_element_type=jnp.float32) * (HEAD_DIM ** -0.5)
    if mask is not None:
        s = jnp.where(mask, s, NEG_INF)
    sink_col = jnp.broadcast_to(sink.astype(jnp.float32).reshape(1, N_KV_HEADS, Q_PER_KV, 1, 1),
                                s.shape[:-1] + (1,))
    p = jax.nn.softmax(jnp.concatenate([s, sink_col], axis=-1), axis=-1)[..., :-1]
    return jnp.einsum('bhgqk,bkhd->bqhgd', p.astype(v.dtype), v)

def _banded_window_attention(q, k, v, kc, vc, sink):
    B, L = q.shape[:2]
    n_blocks = L // BLOCK
    qb = q.reshape(B, n_blocks, BLOCK, N_KV_HEADS, Q_PER_KV, HEAD_DIM)
    pad = ((0, 0), (BLOCK, BLOCK), (0, 0), (0, 0))
    kp, vp = jnp.pad(k, pad), jnp.pad(v, pad)
    r = jnp.arange(BLOCK)
    cidx = jnp.arange(3 * BLOCK)
    band = jnp.abs((cidx[None, :] - BLOCK) - r[:, None]) <= WINDOW
    ctx_cols = jnp.ones((BLOCK, kc.shape[1]), dtype=bool)

    def one_block(i):
        q_i = lax.dynamic_index_in_dim(qb, i, axis=1, keepdims=False)
        k_i = lax.dynamic_slice_in_dim(kp, i * BLOCK, 3 * BLOCK, axis=1)
        v_i = lax.dynamic_slice_in_dim(vp, i * BLOCK, 3 * BLOCK, axis=1)
        kpos = i * BLOCK - BLOCK + cidx
        inside = (kpos >= 0) & (kpos < L)
        mask = jnp.concatenate([band & inside[None, :], ctx_cols], axis=1)
        return _sink_attention(q_i, jnp.concatenate([k_i, kc], axis=1),
                               jnp.concatenate([v_i, vc], axis=1), sink, mask)

    o = lax.map(one_block, jnp.arange(n_blocks))
    return jnp.moveaxis(o, 0, 1).reshape(B, L, ATTN_DIM)

def _multiscale_pool(u, pool_w, pool_scale):
    T = u.shape[1]
    uf = u.astype(jnp.float32)
    cs = jnp.concatenate([jnp.zeros_like(uf[:, :1]), jnp.cumsum(uf, axis=1)], axis=1)
    t = jnp.arange(T)
    diffs = []
    for g, w in enumerate(POOL_WINDOWS):
        sl = slice(g * POOL_GROUP_DIM, (g + 1) * POOL_GROUP_DIM)
        lo = jnp.clip(t - w // 2, 0, T)
        hi = jnp.clip(t + w // 2, 0, T)
        cnt = (hi - lo).astype(jnp.float32)[:, None]
        diffs.append((cs[:, hi, sl] - cs[:, lo, sl]) / cnt - uf[..., sl])
    d = jnp.stack(diffs, axis=2).astype(u.dtype)
    y = jnp.einsum('btgi,gio->btgo', d, pool_w)
    return y.reshape(u.shape) * pool_scale

def _split_ap(z):
    return jnp.split(z, [ATTN_DIM, ATTN_DIM + KV_DIM, ATTN_DIM + 2 * KV_DIM,
                         ATTN_DIM + 2 * KV_DIM + POOL_DIM], axis=-1)

def _ap_output(attn, u, gz, pool_w, pool_scale, w_out):
    y = jnp.concatenate([attn, _multiscale_pool(u, pool_w, pool_scale)], axis=-1) * jax.nn.silu(gz)
    return y @ w_out

def _attn_pool_layer(x, xc, c, c_ctx, cos, sin, ada_w, ada_b, norm_g, w_in, w_out, sink,
                     pool_w, pool_scale, update_ctx):
    B, L = x.shape[:2]
    h, gate = _modulate(x, c[:, None, :], ada_w, ada_b, norm_g)
    hc, gate_c = _modulate(xc, c_ctx, ada_w, ada_b, norm_g)
    q, k, v, u, gz = _split_ap(h @ w_in)
    q = _rope(_heads(q, N_Q_HEADS), cos, sin).reshape(B, L, N_KV_HEADS, Q_PER_KV, HEAD_DIM)
    k = _rope(_heads(k, N_KV_HEADS), cos, sin)
    v = _heads(v, N_KV_HEADS)
    if update_ctx:
        qc, kc, vc, uc, gzc = _split_ap(hc @ w_in)
    else:
        kc, vc = jnp.split(hc @ w_in[:, ATTN_DIM:ATTN_DIM + 2 * KV_DIM], 2, axis=-1)
    kc, vc = _heads(kc, N_KV_HEADS), _heads(vc, N_KV_HEADS)
    attn = _banded_window_attention(q, k, v, kc, vc, sink)
    x_new = x + gate * _ap_output(attn, u, gz, pool_w, pool_scale, w_out)
    if update_ctx:
        Lc = xc.shape[1]
        qc = _heads(qc, N_Q_HEADS).reshape(B, Lc, N_KV_HEADS, Q_PER_KV, HEAD_DIM)
        attn_c = _sink_attention(qc, kc, vc, sink).reshape(B, Lc, ATTN_DIM)
        xc = xc + gate_c * _ap_output(attn_c, uc, gzc, pool_w, pool_scale, w_out)
    return x_new, xc

def _depthwise_conv(u, w, b):
    y = lax.conv_general_dilated(u, w[:, None, :].astype(u.dtype), window_strides=(1,),
                                 padding=((CONV_K // 2, CONV_K // 2),),
                                 dimension_numbers=('NWC', 'WIO', 'NWC'),
                                 feature_group_count=u.shape[-1])
    return y + b

def _conformer_conv_mixer(z, dw_w, dw_b, ln_g, ln_b, w_out):
    a, b, gz = jnp.split(z, 3, axis=-1)
    u = a * jax.nn.sigmoid(b)
    u = jax.nn.silu(_layernorm(_depthwise_conv(u, dw_w, dw_b), ln_g, ln_b))
    return (u * jax.nn.silu(gz)) @ w_out

def _conv_layer(x, xc, c, c_ctx, ada_w, ada_b, norm_g, w_in, w_out, dw_w, dw_b, ln_g, ln_b, update_ctx):
    h, gate = _modulate(x, c[:, None, :], ada_w, ada_b, norm_g)
    x_new = x + gate * _conformer_conv_mixer(h @ w_in, dw_w, dw_b, ln_g, ln_b, w_out)
    if update_ctx:
        hc, gate_c = _modulate(xc, c_ctx, ada_w, ada_b, norm_g)
        xc = xc + gate_c * _conformer_conv_mixer(hc @ w_in, dw_w, dw_b, ln_g, ln_b, w_out)
    return x_new, xc

def setup_inputs(seed: int = 0) -> dict:
    key = jax.random.key(seed)
    ks = jax.random.split(key, 22)
    D = D_MODEL

    def nrm(k, shape, s):
        return s * jax.random.normal(k, shape, jnp.float32)

    return {
        "x": nrm(ks[0], (BATCH, SEQ, D), 1.0),
        "c": nrm(ks[1], (BATCH, D), 1.0),
        "ctx": nrm(ks[2], (BATCH, CTX_LEN, D), 1.0),
        "c_ctx": nrm(ks[3], (D,), 1.0),
        "ap_ada_w": nrm(ks[4], (N_AP_LAYERS, D, 3 * D), 0.3 * D ** -0.5),
        "ap_ada_b": nrm(ks[5], (N_AP_LAYERS, 3 * D), 0.02),
        "ap_norm_g": 1.0 + nrm(ks[6], (N_AP_LAYERS, D), 0.05),
        "ap_w_in": nrm(ks[7], (N_AP_LAYERS, D, AP_IN_DIM), D ** -0.5),
        "ap_w_out": nrm(ks[8], (N_AP_LAYERS, AP_GATE_DIM, D), AP_GATE_DIM ** -0.5),
        "ap_sink": nrm(ks[9], (N_AP_LAYERS, N_Q_HEADS), 0.5),
        "ap_pool_w": nrm(ks[10], (N_AP_LAYERS, len(POOL_WINDOWS), POOL_GROUP_DIM, POOL_GROUP_DIM),
                          POOL_GROUP_DIM ** -0.5),
        "ap_pool_scale": 1.0 + nrm(ks[11], (N_AP_LAYERS, POOL_DIM), 0.1),
        "cv_ada_w": nrm(ks[12], (N_CV_LAYERS, D, 3 * D), 0.3 * D ** -0.5),
        "cv_ada_b": nrm(ks[13], (N_CV_LAYERS, 3 * D), 0.02),
        "cv_norm_g": 1.0 + nrm(ks[14], (N_CV_LAYERS, D), 0.05),
        "cv_w_in": nrm(ks[15], (N_CV_LAYERS, D, CV_IN_DIM), D ** -0.5),
        "cv_w_out": nrm(ks[16], (N_CV_LAYERS, CONV_DIM, D), CONV_DIM ** -0.5),
        "cv_dw_w": nrm(ks[17], (N_CV_LAYERS, CONV_K, CONV_DIM), CONV_K ** -0.5),
        "cv_dw_b": nrm(ks[18], (N_CV_LAYERS, CONV_DIM), 0.02),
        "cv_ln_g": 1.0 + nrm(ks[19], (N_CV_LAYERS, CONV_DIM), 0.05),
        "cv_ln_b": nrm(ks[20], (N_CV_LAYERS, CONV_DIM), 0.02),
        "final_norm_g": 1.0 + nrm(ks[21], (D,), 0.05),
    }

def reference(x, c, ctx, c_ctx, ap_ada_w, ap_ada_b, ap_norm_g, ap_w_in, ap_w_out, ap_sink,
              ap_pool_w, ap_pool_scale, cv_ada_w, cv_ada_b, cv_norm_g, cv_w_in, cv_w_out,
              cv_dw_w, cv_dw_b, cv_ln_g, cv_ln_b, final_norm_g):
    L = x.shape[1]
    cos, sin = _axial_rope_tables(L)
    last_ap_layer = ((DEPTH - 1) // 2) * 2
    xc = ctx
    for i in range(DEPTH):
        j = i // 2
        update_ctx = i < last_ap_layer
        if i % 2 == 0:
            x, xc = _attn_pool_layer(x, xc, c, c_ctx, cos, sin, ap_ada_w[j], ap_ada_b[j], ap_norm_g[j],
                                     ap_w_in[j], ap_w_out[j], ap_sink[j], ap_pool_w[j],
                                     ap_pool_scale[j], update_ctx)
        else:
            x, xc = _conv_layer(x, xc, c, c_ctx, cv_ada_w[j], cv_ada_b[j], cv_norm_g[j], cv_w_in[j],
                                cv_w_out[j], cv_dw_w[j], cv_dw_b[j], cv_ln_g[j], cv_ln_b[j], update_ctx)
    return _rmsnorm(x, final_norm_g)


_drawn_inputs = setup_inputs


def setup_inputs(seed=0):
    import zlib

    import numpy as np

    out = dict(_drawn_inputs(seed))
    spreads = {}
    factors = {'ctx': 8.0,
     'c_ctx': 8.0,
     'ap_ada_b': 6.704,
     'ap_norm_g': 8.0,
     'ap_sink': 8.0,
     'ap_pool_scale': 7.725,
     'cv_ada_b': 7.186,
     'cv_norm_g': 34.893,
     'cv_dw_b': 64.0,
     'cv_ln_g': 60.704,
     'cv_ln_b': 179.756}
    for name, (base, spread) in spreads.items():
        noise = np.random.default_rng([zlib.crc32(name.encode()), seed]).standard_normal(out[name].shape)
        drawn = base * np.exp(spread * noise) if base else spread * noise
        out[name] = __import__('jax').numpy.asarray(drawn.astype(out[name].dtype))
    for name, factor in factors.items():
        out[name] = (out[name] * factor).astype(out[name].dtype)
    return out
```

```python
import numpy as np
import concourse.bass as bass
from concourse import mybir
from contextlib import ExitStack

F32 = mybir.dt.float32
F32R = mybir.dt.float32r
BF16 = mybir.dt.bfloat16
I32 = mybir.dt.int32
ALU = mybir.AluOpType
ACT = mybir.ActivationFunctionType
AXIS = mybir.AxisListType

P = 128
D = 1024
KT = D // P
SEQ = 4096
CTX = 256
GRID_W = 64
HD = 64
NQ = 8
NKV = 2
GRP = NQ // NKV
ATTN = NQ * HD
KV = NKV * HD
POOL_WINDOWS = (2, 4, 8, 16)
POOL = D - ATTN
CONV_K = 31
HALO = CONV_K // 2
EPS = 1e-6
NEG = -1e30
SCALE = HD ** -0.5
QKV = ATTN + 2 * KV
WIN = 3 * P
KEYS = WIN + CTX
CW = 512
NCH = SEQ // CW
TPC = CW // P
TILES = SEQ // P
KPAD = CTX + P + SEQ + P
PHALO = max(POOL_WINDOWS) // 2
UPAD = SEQ + 2 * PHALO
CPAD = SEQ + 2 * HALO
PAIR = 2 * CW
RSQRT_MAGIC = 0x5F3759DF
RSQRT_STEPS = 14


def rope_tables():
    rows = SEQ // GRID_W
    pairs = HD // 4
    row = np.repeat(np.arange(rows, dtype=np.float32), GRID_W)
    col = np.tile(np.arange(GRID_W, dtype=np.float32), rows)
    inv = np.float32(10000.0) ** (-np.arange(pairs, dtype=np.float32) / np.float32(pairs))
    ang = np.concatenate([row[:, None] * inv, col[:, None] * inv], axis=-1).astype(np.float32)
    cs = np.concatenate([np.ones((CTX, HD // 2), np.float32), np.cos(ang)])
    sn = np.concatenate([np.zeros((CTX, HD // 2), np.float32), np.sin(ang)])
    return np.stack([cs, sn], axis=1).astype(np.float32)


def pool_counts():
    t = np.arange(SEQ)
    out = [1.0 / (np.clip(t + w // 2, 0, SEQ) - np.clip(t - w // 2, 0, SEQ)) for w in POOL_WINDOWS]
    return np.stack(out).astype(np.float32)


def band_masks():
    r = np.arange(P)[:, None]
    c = np.arange(WIN)[None, :]
    inner = np.where(np.abs(c - P - r) <= P, 0.0, NEG)
    first = np.where(c < P, NEG, inner)
    last = np.where(c >= 2 * P, NEG, inner)
    return np.stack([first, inner, last], axis=1).astype(np.float32)


def build(nc, x, c, ctx_in, c_ctx, ap_ada_w, ap_ada_b, ap_norm_g, ap_w_in, ap_w_out, ap_sink,
          ap_pool_w, ap_pool_scale, cv_ada_w, cv_ada_b, cv_norm_g, cv_w_in, cv_w_out, cv_dw_w,
          cv_dw_b, cv_ln_g, cv_ln_b, final_norm_g, rope, counts, masks, out):
    scratch = lambda name, shape: nc.dram_tensor(name, shape, F32).ap()
    qT_d = scratch("qT_d", [NQ, P, CTX + SEQ])
    kT_d = scratch("kT_d", [2 * NKV, P, KPAD])
    v_d = scratch("v_d", [KPAD, 2, KV])
    aT_d = scratch("aT_d", [ATTN, SEQ])
    uT_d = scratch("uT_d", [POOL, UPAD])
    gT_d = scratch("gT_d", [D, SEQ])
    x1_d = scratch("x1_d", [SEQ, D])
    gate_d = scratch("gate_d", [2, D])
    cuT_d = scratch("cuT_d", [D, CPAD])
    ccT_d = scratch("ccT_d", [D, SEQ])
    cgT_d = scratch("cgT_d", [D, SEQ])

    whole = ExitStack()
    with whole:
        def persistent(name, shape, dt=F32):
            return whole.enter_context(nc.sbuf_tensor(name, shape, dt))

        ident = persistent("ident", [P, P])
        ident16 = persistent("ident16", [P, P], BF16)
        G = persistent("G", [P, 3, KT])
        S = persistent("S", [P, 3, KT])
        rstd0 = persistent("rstd0", [P, (CTX + SEQ) // P])
        rstd1 = persistent("rstd1", [P, TILES])

        used = []

        def new_sem(stack, name):
            handle = stack.enter_context(nc.semaphore(name))
            used.append(handle)
            return handle

        def clear_semaphores():
            with nc.Block() as block:
                @block.gpsimd
                def _(pool):
                    for handle in used:
                        pool.sem_clear(handle)
            used.clear()

        def rsqrt(dve, step, n0, dst, v, tmp):
            n = n0

            def then(ins):
                nonlocal n
                ins.then_inc(step, 1)
                n = n + 1
                dve.wait_ge(step, n)

            then(dve.tensor_scalar(tmp.bitcast(I32), v.bitcast(I32), 1, None, ALU.logical_shift_right))
            then(dve.tensor_scalar(dst.bitcast(I32), tmp.bitcast(I32), -1.0, float(RSQRT_MAGIC), ALU.mult, ALU.add))
            for _ in range(3):
                then(dve.tensor_tensor(tmp, dst, dst, ALU.mult))
                then(dve.tensor_tensor(tmp, tmp, v, ALU.mult))
                then(dve.tensor_scalar(tmp, tmp, -0.5, 1.5, ALU.mult, ALU.add))
                then(dve.tensor_tensor(dst, dst, tmp, ALU.mult))

        def product(pe, acc, left, right, first, last):
            (lh, ll), (rh, rl) = left, right
            pe.matmul(acc, lh, rh, start=first, stop=False)
            pe.matmul(acc, lh, rl, start=False, stop=False)
            return pe.matmul(acc, ll, rh, start=False, stop=last)

        def f32v(ap):
            return ap.bitcast(F32)

        with ExitStack() as stage:
            sb = lambda n, s, d=F32: stage.enter_context(nc.sbuf_tensor(n, s, d))
            ps = lambda n, s, d=F32: stage.enter_context(nc.psum_tensor(n, s, d))
            sem = lambda n: new_sem(stage, n)
            zeros = sb("zeros", [P, 2 * KV])
            cond = sb("cond", [P, KT, 2])
            scond = sb("scond", [P, KT, 2])
            adab = sb("adab", [P, 2, 2 * KT])
            normg = sb("normg", [P, 2, KT])
            gbias = sb("gbias", [1, 2, D])
            gate = sb("gate", [1, 2, D])
            shsc = sb("shsc", [P, 2, 2 * KT, 2])
            NAS = 4
            adaw = sb("adaw", [P, NAS, 3 * D])
            cols_ps = ps("cols_ps", [P, 2, 512])
            gate_ps = ps("gate_ps", [1, 2, 512])
            small_loaded = sem("small_loaded")
            zeroed = sem("zeroed")
            padded = sem("padded")
            ident_made = sem("ident_made")
            cond_ready = sem("cond_ready")
            adaw_loaded = [sem(f"adaw_loaded{i}") for i in range(NAS)]
            adaw_free = sem("adaw_free")
            cols_ready = sem("cols_ready")
            gate_stored = sem("gate_stored")
            cols_free = sem("cols_free")
            vec_step = sem("vec_step")
            block = stage.enter_context(nc.Block())

            @block.sync
            def _(sp):
                for r, src in enumerate((ap_ada_w, cv_ada_w)):
                    for k in range(KT):
                        n = r * KT + k
                        sp.wait_ge(adaw_free, n + 1)
                        sp.dma_start(adaw[:, n % NAS, :], src[0, k * P:(k + 1) * P, :]).then_inc(adaw_loaded[n % NAS], 16)
                sp.wait_ge(vec_step, 4)
                sp.dma_start(gate_d.rearrange("(a r) d -> a r d", a=1), gate[:]).then_inc(gate_stored, 16)
                sp.wait_ge(gate_stored, 16)

            @block.gpsimd
            def _(pool):
                pool.memset(ident[:], 0.0).then_inc(ident_made, 1)
                pool.memset(ident16[:], 0.0).then_inc(ident_made, 1)
                pool.wait_ge(ident_made, 2)
                for m in (ident, ident16):
                    pool.affine_select(out=m[:], in_=m[:], compare_op=ALU.not_equal, fill=1.0, base=0,
                                       pattern=[[-1, P]], channel_multiplier=1).then_inc(ident_made, 1)
                pool.memset(zeros[:], 0.0).then_inc(zeroed, 1)
                pool.wait_ge(zeroed, 1)

            @block.scalar
            def _(act):
                by_channel = lambda v: v.rearrange("(k p) -> p k", p=P)
                smalls = [(cond[:, :, 0], by_channel(c[0, :])), (cond[:, :, 1], by_channel(c_ctx)),
                          (adab[:, 0, :], by_channel(ap_ada_b[0, 0:2 * D])), (adab[:, 1, :], by_channel(cv_ada_b[0, 0:2 * D])),
                          (normg[:, 0, :], by_channel(ap_norm_g[0, :])), (normg[:, 1, :], by_channel(cv_norm_g[0, :])),
                          (gbias[:, 0, :], ap_ada_b[0:1, 2 * D:3 * D]),
                          (gbias[:, 1, :], cv_ada_b[0:1, 2 * D:3 * D])]
                for dst, src in smalls:
                    act.dma_start(dst, src, allow_slow_non_contiguous=True).then_inc(small_loaded, 16)
                act.wait_ge(small_loaded, 16 * len(smalls))
                act.activation(scond[:], cond[:], ACT.Silu).then_inc(cond_ready, 1)
                act.wait_ge(zeroed, 1)
                pads = []
                for at in (CTX, CTX + P + SEQ):
                    pads += [(kT_d[n, :, at:at + P], zeros[:, 0:P]) for n in range(2 * NKV)]
                    pads += [(v_d[at:at + P, :, :], zeros[:].rearrange("p (a d) -> p a d", a=2))]
                for t in range(POOL // P):
                    for at in (0, PHALO + SEQ):
                        pads.append((uT_d[t * P:(t + 1) * P, at:at + PHALO], zeros[:, 0:PHALO]))
                for t in range(KT):
                    for at in (0, HALO + SEQ):
                        pads.append((cuT_d[t * P:(t + 1) * P, at:at + HALO], zeros[:, 0:HALO]))
                for dst, src in pads:
                    act.dma_start(dst, src).then_inc(padded, 16)
                act.wait_ge(padded, 16 * len(pads))

            @block.tensor
            def _(pe):
                pe.sem_inc(adaw_free, NAS)
                pe.wait_ge(cond_ready, 1)
                for r in range(2):
                    for k in range(KT):
                        n = r * KT + k
                        slot = n % NAS
                        pe.wait_ge(adaw_loaded[slot], 16 * (n // NAS + 1))
                        if n >= 2:
                            pe.wait_ge(cols_free, n - 1)
                        for t in range(2 * KT):
                            last = pe.matmul(cols_ps[:, n % 2, 2 * t:2 * t + 2], adaw[:, slot, t * P:(t + 1) * P],
                                             scond[:, k, :], start=True, stop=True)
                        last.then_inc(cols_ready, 1)
                        if n == KT:
                            pe.wait_ge(vec_step, 2)
                        for h in range(2):
                            last = pe.matmul(gate_ps[:, h, :], scond[:, k, 0:1], adaw[:, slot, 2 * D + 512 * h:2 * D + 512 * (h + 1)],
                                             start=(k == 0), stop=(k == KT - 1))
                        last.then_inc(adaw_free, 1)

            @block.vector
            def _(dve):
                dve.wait_ge(small_loaded, 16 * 8)
                for r in range(2):
                    for k in range(KT):
                        n = r * KT + k
                        dve.wait_ge(cols_ready, n + 1)
                        src = cols_ps[:, n % 2, 0:4 * KT].rearrange("p (t v) -> p t v", v=2)
                        if k == 0:
                            dve.tensor_copy(shsc[:, r], src).then_inc(cols_free, 1)
                        else:
                            dve.wait_ge(cols_free, n)
                            dve.tensor_tensor(shsc[:, r], shsc[:, r], src, ALU.add).then_inc(cols_free, 1)
                    dve.wait_ge(adaw_free, NAS + (r + 1) * KT)
                    for h in range(2):
                        dve.tensor_tensor(gate[:, r, 512 * h:512 * (h + 1)], gate_ps[:, h, :],
                                          gbias[:, r, 512 * h:512 * (h + 1)], ALU.add).then_inc(vec_step, 1)
                dve.wait_ge(cols_free, 2 * KT)
                dve.wait_ge(small_loaded, 16 * 8)
                step = 4
                for m, (r, v) in enumerate(((0, 0), (0, 1), (1, 0))):
                    dve.tensor_tensor(S[:, m, :], shsc[:, r, 0:KT, v], adab[:, r, 0:KT], ALU.add)
                    dve.tensor_tensor(G[:, m, :], shsc[:, r, KT:2 * KT, v], adab[:, r, KT:2 * KT], ALU.add).then_inc(vec_step, 1)
                    step += 1
                    dve.wait_ge(vec_step, step)
                    dve.scalar_tensor_tensor(G[:, m, :], G[:, m, :], 1.0, normg[:, r, :], ALU.add, ALU.mult).then_inc(vec_step, 1)
                    step += 1
                dve.wait_ge(vec_step, step)

        def split_weights(name, pieces, hi, lo, scale_by=None):
            width = sum(w for _, _, w in pieces)
            with ExitStack() as stage:
                raw = stage.enter_context(nc.sbuf_tensor(name + "_raw", [P, 3, width], F32))
                loaded = [new_sem(stage, f"{name}_loaded{i}") for i in range(3)]
                raw_free = new_sem(stage, name + "_raw_free")
                hi_ready = new_sem(stage, name + "_hi_ready")
                scaled = new_sem(stage, name + "_scaled")
                if scale_by is not None:
                    row, row_loaded, row_src = scale_by
                block = stage.enter_context(nc.Block())
                n_k = hi.shape[1]

                @block.sync
                def _(sp):
                    sp.sem_inc(raw_free, 3)
                    if scale_by is not None:
                        sp.dma_start(row[:], row_src).then_inc(row_loaded, 16)
                    for k in range(n_k):
                        sp.wait_ge(raw_free, k + 1)
                        for at, src, w in pieces:
                            sp.dma_start(raw[:, k % 3, at:at + w], src(k)).then_inc(loaded[k % 3], 16)

                @block.scalar
                def _(act):
                    for k in range(n_k):
                        act.wait_ge(loaded[k % 3], 16 * len(pieces) * (k // 3 + 1))
                        if scale_by is not None:
                            act.wait_ge(scaled, k + 1)
                        act.activation(hi[:, k, :], raw[:, k % 3, :], ACT.Copy).then_inc(hi_ready, 1)

                @block.vector
                def _(dve):
                    def fold(k):
                        dve.wait_ge(loaded[k % 3], 16 * len(pieces) * (k // 3 + 1))
                        dve.tensor_tensor(raw[:, k % 3, :], raw[:, k % 3, :], row[:], ALU.mult).then_inc(scaled, 1)

                    if scale_by is not None:
                        dve.wait_ge(row_loaded, 16)
                        fold(0)
                    for k in range(n_k):
                        if scale_by is not None and k + 1 < n_k:
                            fold(k + 1)
                        dve.wait_ge(hi_ready, k + 1)
                        dve.tensor_tensor(lo[:, k, :], raw[:, k % 3, :], f32v(hi[:, k, :]), ALU.subtract).then_inc(raw_free, 1)

        def chunks(eng, body, count, head, tail):
            for n in range(head):
                body(n, n % 2, n, count - 1 - n)
            with eng.Fori(0, (count - head - tail) // 2) as i:
                for n in (head, head + 1):
                    body(i * 2 + n, n % 2, n, tail)
            for n in range(count - tail, count):
                body(n, n % 2, n, count - 1 - n)

        turns = whole.enter_context(nc.semaphore("turns"))

        def at_turn(sp, sem, value):
            sp.wait_ge(sem, value)
            sp.sem_inc(turns, 1)

        clear_semaphores()
        with ExitStack() as stage:
            sb = lambda n, s, d=F32: stage.enter_context(nc.sbuf_tensor(n, s, d))
            ps = lambda n, s, d=F32: stage.enter_context(nc.psum_tensor(n, s, d))
            sem = lambda n: new_sem(stage, n)
            w_hi = sb("qkv_w_hi", [P, KT, QKV], F32R)
            w_lo = sb("qkv_w_lo", [P, KT, QKV], F32R)
            split_weights("qkv_w", [(0, lambda k: ap_w_in[0, k * P:(k + 1) * P, 0:QKV], QKV)], w_hi, w_lo)
            T2 = 256
            SUB = T2 // P
            NH = NQ + NKV
            xin = sb("s1_x", [P, 2, SUB, D])
            junk = sb("s1_junk", [P, D])
            ss = sb("s1_ss", [P, 2, SUB])
            var = sb("s1_var", [P, SUB])
            tmp = sb("s1_tmp", [P, SUB])
            cs = sb("s1_rope", [P, 2, SUB, 2, HD // 2])
            xT = sb("s1_xT", [P, KT, T2])
            xT_hi = sb("s1_xT_hi", [P, 2, KT, T2], F32R)
            xT_lo = sb("s1_xT_lo", [P, 2, KT, T2], F32R)
            rot_c = sb("s1_rot_c", [P, NH, 2, HD // 2])
            rot_s = sb("s1_rot_s", [P, NH, 2, HD // 2])
            rot = sb("s1_rot", [P, NH, 2, HD // 2])
            q_sp = sb("s1_q_sp", [P, 2, NQ, 2, HD], F32R)
            k_sp = sb("s1_k_sp", [P, 2, 2, NKV, 2, HD], F32R)
            v_sp = sb("s1_v_sp", [P, 2, 2, KV], F32R)
            NT = NQ + 2 * NKV
            qk_t = sb("s1_qk_t", [P, 2, NT, P])
            tr_ps = ps("s1_tr_ps", [P, 2, 2, T2])
            qkv_ps = ps("s1_qkv_ps", [P, 2, 2, 512])
            out_ps = ps("s1_out_ps", [P, 2, 4, P])
            x_loaded = [sem(f"s1_x_loaded{i}") for i in range(2)]
            rope_loaded = [sem(f"s1_rope_loaded{i}") for i in range(2)]
            ss_ready = sem("s1_ss_ready")
            rs_step = sem("s1_rs_step")
            xn_ready = sem("s1_xn_ready")
            tr_ready = sem("s1_tr_ready")
            xT_ready = sem("s1_xT_ready")
            hi_ready = sem("s1_hi_ready")
            split_ready = sem("s1_split_ready")
            qkv_ready = sem("s1_qkv_ready")
            rot_step = sem("s1_rot_step")
            v_ready = sem("s1_v_ready")
            heads_split = sem("s1_heads_split")
            v_stored = [sem(f"s1_v_stored{i}") for i in range(2)]
            heads_ready = sem("s1_heads_ready")
            heads_out = sem("s1_heads_out")
            heads_stored = [sem(f"s1_heads_stored{i}") for i in range(2)]
            block = stage.enter_context(nc.Block())
            CHUNKS = 1 + SEQ // T2
            HEAD, TAIL = 3, 2
            BANKS = KT // 2
            OUTS = NT // 4

            @block.sync
            def _(sp):
                def load(n, slot, before):
                    if before >= 2:
                        at_turn(sp, tr_ready, (n - 1) * BANKS)
                    src = ctx_in[0, :, :] if before == 0 else x[0, bass.ds((n - 1) * T2, T2), :]
                    sp.dma_start(xin[:, slot], src.rearrange("(s p) d -> p s d", p=P)).then_inc(x_loaded[slot], 16)

                def load_rope(n, slot, before):
                    if before >= 2:
                        at_turn(sp, heads_split, (n - 1) * SUB)
                    sp.dma_start(cs[:, slot], rope[bass.ds(n * T2, T2), :, :].rearrange("(s p) a d -> p s a d", p=P)).then_inc(rope_loaded[slot], 16)

                def store(n, s, is_ctx):
                    u = n * SUB + s
                    col = n * T2 + s * P
                    key = col + (0 if is_ctx else P)
                    at_turn(sp, v_ready, u + 1)
                    sp.dma_start(v_d[bass.ds(key, P), :, :], f32v(v_sp[:, s])).then_inc(v_stored[s], 16)
                    at_turn(sp, heads_out, (u + 1) * OUTS)
                    sp.dma_start(qT_d[:, :, bass.ds(col, P)].rearrange("h p t -> p h t"), qk_t[:, s, 0:NQ, :]).then_inc(heads_stored[s], 16)
                    sp.dma_start(kT_d[:, :, bass.ds(key, P)].rearrange("h p t -> p h t"), qk_t[:, s, NQ:NT, :]).then_inc(heads_stored[s], 16)

                def body(n, slot, before, after):
                    if before == 0:
                        load(0, 0, 0)
                        load(1, 1, 1)
                        load_rope(0, 0, 0)
                    if after >= 2:
                        load(n + 2, slot, before + 2)
                    if after >= 1:
                        load_rope(n + 1, 1 - slot, before + 1)
                    if before >= 1:
                        store(n - 1, 1, before == 1)
                    store(n, 0, before == 0)

                chunks(sp, body, CHUNKS, HEAD, TAIL)
                store(CHUNKS - 1, 1, False)
                for s in range(SUB):
                    sp.wait_ge(v_stored[s], 16 * CHUNKS)
                    sp.wait_ge(heads_stored[s], 32 * CHUNKS)

            @block.scalar
            def _(act):
                def squares(n, slot, before):
                    act.wait_ge(x_loaded[slot], 8 * (n + 2 - slot))
                    for s in range(SUB):
                        if before + s > 0:
                            act.wait_ge(ss_ready, n * SUB + s)
                        act.activation(junk[:], xin[:, slot, s, :], ACT.Square,
                                       accum_out=ss[:, slot, s:s + 1]).then_inc(ss_ready, 1)

                def evacuate_xT(n, before):
                    which = 1 if before == 0 else 0
                    for b in range(BANKS):
                        act.wait_ge(tr_ready, n * BANKS + b + 1)
                        if b == 0 and before >= 1:
                            act.wait_ge(split_ready, 2 * n)
                        for kk in range(2):
                            k = 2 * b + kk
                            ins = act.activation(xT[:, k, :], tr_ps[:, b % 2, kk, :], ACT.Identity,
                                                 scale=G[:, which, k:k + 1], bias=S[:, which, k:k + 1])
                        ins.then_inc(xT_ready, 1)

                def evacuate_heads(n, s, before):
                    u = n * SUB + s
                    if before >= 1:
                        act.wait_ge(heads_stored[s], 32 * n)
                    for b in range(OUTS):
                        act.wait_ge(heads_ready, u * OUTS + b + 1)
                        act.activation(qk_t[:, s, 4 * b:4 * b + 4, :], out_ps[:, (s * OUTS + b) % 2], ACT.Copy).then_inc(heads_out, 1)

                def body(n, slot, before, after):
                    if before == 0:
                        squares(0, 0, 0)
                        squares(1, 1, 1)
                        evacuate_xT(0, 0)
                    if before >= 1:
                        evacuate_heads(n - 1, 1, before - 1)
                    if after >= 1:
                        evacuate_xT(n + 1, before + 1)
                    if after >= 2:
                        squares(n + 2, slot, before + 2)
                    evacuate_heads(n, 0, before)

                chunks(act, body, CHUNKS, HEAD, TAIL)
                evacuate_heads(CHUNKS - 1, 1, 9)

            @block.vector
            def _(dve):
                def normalise(n, slot, before):
                    if before >= 1:
                        dve.wait_ge(xn_ready, n)
                    dve.wait_ge(ss_ready, (n + 1) * SUB)
                    dve.tensor_scalar(var[:], ss[:, slot, :], 1.0 / D, EPS, ALU.mult, ALU.add).then_inc(rs_step, 1)
                    step = n * (RSQRT_STEPS + 1) + 1
                    dve.wait_ge(rs_step, step)
                    rs = rstd0[:, bass.ds(n * SUB, SUB)]
                    rsqrt(dve, rs_step, step, rs, var[:], tmp[:])
                    for s in range(SUB):
                        ins = dve.tensor_scalar(xin[:, slot, s, :], xin[:, slot, s, :], rstd0[:, bass.ds(n * SUB + s, 1)], None, ALU.mult)
                    ins.then_inc(xn_ready, 1)

                def split(n, slot, before):
                    if before >= 2:
                        dve.wait_ge(qkv_ready, (n - 1) * SUB)
                    for h in range(2):
                        ks = slice(4 * h, 4 * h + 4)
                        dve.wait_ge(xT_ready, n * BANKS + 2 * h + 2)
                        dve.tensor_copy(xT_hi[:, slot, ks], xT[:, ks]).then_inc(hi_ready, 1)
                        dve.wait_ge(hi_ready, n * 2 + h + 1)
                        dve.tensor_tensor(xT_lo[:, slot, ks], xT[:, ks], f32v(xT_hi[:, slot, ks]), ALU.subtract).then_inc(split_ready, 1)

                def rotate(n, slot, s, before):
                    u = n * SUB + s
                    q_in = qkv_ps[:, s, 0, :].rearrange("p (h a d) -> p h a d", a=2, d=HD // 2)
                    k_in = qkv_ps[:, s, 1, 0:KV].rearrange("p (h a d) -> p h a d", a=2, d=HD // 2)
                    v_in = qkv_ps[:, s, 1, KV:2 * KV]
                    dve.wait_ge(qkv_ready, u + 1)
                    dve.wait_ge(rope_loaded[slot], 8 * (n + 2 - slot))
                    if before >= 1:
                        dve.wait_ge(v_stored[s], 16 * n)
                    if before + s >= 1:
                        dve.wait_ge(heads_split, u)
                    for a, dst in ((0, rot_c), (1, rot_s)):
                        table = cs[:, slot, s, a, :].unsqueeze(1).unsqueeze(1)
                        dve.tensor_tensor(dst[:, 0:NQ], q_in, table.to_broadcast([P, NQ, 2, HD // 2]), ALU.mult)
                        dve.tensor_tensor(dst[:, NQ:NH], k_in, table.to_broadcast([P, NKV, 2, HD // 2]), ALU.mult)
                    dve.tensor_copy(v_sp[:, s, 0, :], v_in).then_inc(rot_step, 1)
                    dve.wait_ge(rot_step, u * 3 + 1)
                    dve.tensor_tensor(v_sp[:, s, 1, :], v_in, f32v(v_sp[:, s, 0, :]), ALU.subtract).then_inc(v_ready, 1)
                    dve.tensor_tensor(rot[:, :, 0, :], rot_c[:, :, 0, :], rot_s[:, :, 1, :], ALU.subtract)
                    dve.tensor_tensor(rot[:, :, 1, :], rot_c[:, :, 1, :], rot_s[:, :, 0, :], ALU.add).then_inc(rot_step, 1)
                    dve.wait_ge(rot_step, u * 3 + 2)
                    if before >= 1:
                        dve.wait_ge(heads_ready, (u - 1) * OUTS)
                    qr = rot[:, 0:NQ].rearrange("p h a d -> p h (a d)")
                    kr = rot[:, NQ:NH].rearrange("p h a d -> p h (a d)").unsqueeze(2).to_broadcast([P, NKV, 2, HD])
                    dve.tensor_copy(q_sp[:, s, :, 0, :], qr)
                    dve.tensor_copy(k_sp[:, s, 0], kr).then_inc(rot_step, 1)
                    dve.wait_ge(rot_step, u * 3 + 3)
                    dve.tensor_tensor(q_sp[:, s, :, 1, :], qr, f32v(q_sp[:, s, :, 0, :]), ALU.subtract)
                    dve.tensor_tensor(k_sp[:, s, 1], kr, f32v(k_sp[:, s, 0]), ALU.subtract).then_inc(heads_split, 1)

                def body(n, slot, before, after):
                    if before == 0:
                        normalise(0, 0, 0)
                        split(0, 0, 0)
                    if after >= 1:
                        normalise(n + 1, 1 - slot, before + 1)
                    rotate(n, slot, 0, before)
                    if after >= 1:
                        split(n + 1, 1 - slot, before + 1)
                    rotate(n, slot, 1, before)

                chunks(dve, body, CHUNKS, HEAD, TAIL)

            @block.tensor
            def _(pe):
                def transpose_x(n, slot, before):
                    pe.wait_ge(xn_ready, n + 1)
                    for b in range(BANKS):
                        if not (before == 0 and b < 2):
                            pe.wait_ge(xT_ready, n * BANKS + b - 1)
                        for kk in range(2):
                            k = 2 * b + kk
                            for s in range(SUB):
                                ins = pe.transpose(tr_ps[:, b % 2, kk, s * P:(s + 1) * P], xin[:, slot, s, k * P:(k + 1) * P], ident[:])
                        ins.then_inc(tr_ready, 1)

                def products(n, slot, s, before):
                    u = n * SUB + s
                    if s == 0:
                        pe.wait_ge(split_ready, 2 * (n + 1))
                    if before >= 1:
                        pe.wait_ge(v_ready, u - 1)
                    ts = slice(s * P, (s + 1) * P)
                    for k in range(KT):
                        x_parts = (xT_hi[:, slot, k, ts], xT_lo[:, slot, k, ts])
                        product(pe, qkv_ps[:, s, 0, :], x_parts, (w_hi[:, k, 0:ATTN], w_lo[:, k, 0:ATTN]), k == 0, k == KT - 1)
                        ins = product(pe, qkv_ps[:, s, 1, 0:2 * KV], x_parts, (w_hi[:, k, ATTN:QKV], w_lo[:, k, ATTN:QKV]), k == 0, k == KT - 1)
                    ins.then_inc(qkv_ready, 1)

                def heads(n, s, before):
                    u = n * SUB + s
                    pe.wait_ge(heads_split, u + 1)
                    for b in range(OUTS):
                        if not (before == 0 and s * OUTS + b < 2):
                            pe.wait_ge(heads_out, u * OUTS + b - 1)
                        for j in range(4):
                            h = 4 * b + j
                            src = q_sp[:, s, h] if h < NQ else k_sp[:, s, (h - NQ) // NKV, (h - NQ) % NKV]
                            ins = pe.transpose(out_ps[:, (s * OUTS + b) % 2, j, :], f32v(src.rearrange("p a d -> p (a d)")), ident[:])
                        ins.then_inc(heads_ready, 1)

                def body(n, slot, before, after):
                    if before == 0:
                        transpose_x(0, 0, 0)
                    products(n, slot, 0, before)
                    if before >= 1:
                        heads(n - 1, 1, before - 1)
                    if after >= 1:
                        transpose_x(n + 1, 1 - slot, before + 1)
                    products(n, slot, 1, before)
                    heads(n, 0, before)

                chunks(pe, body, CHUNKS, HEAD, TAIL)
                heads(CHUNKS - 1, 1, 9)

        clear_semaphores()
        with ExitStack() as stage:
            sb = lambda n, s, d=F32: stage.enter_context(nc.sbuf_tensor(n, s, d))
            ps = lambda n, s, d=F32: stage.enter_context(nc.psum_tensor(n, s, d))
            sem = lambda n: new_sem(stage, n)
            q_in = sb("s2_q_in", [P, 2, NQ, P], F32R)
            k_in = sb("s2_k_in", [P, 2, 2 * NKV, WIN], F32R)
            v_in = sb("s2_v_in", [P, 2, 3, 2, KV], F32R)
            k_ctx = sb("s2_k_ctx", [P, 2 * NKV, CTX], F32R)
            v_ctx = sb("s2_v_ctx", [P, CTX // P, 2, KV], F32R)
            mask_in = sb("s2_mask_in", [P, 3, WIN])
            mask = sb("s2_mask", [P, 3, WIN], BF16)
            sink = sb("s2_sink", [P, NQ])
            neg_sink = sb("s2_neg_sink", [P, NQ])
            row_max = sb("s2_row_max", [P, NQ])
            neg_max = sb("s2_neg_max", [P, NQ])
            p_sum = sb("s2_p_sum", [P, NQ])
            p_sink = sb("s2_p_sink", [P, NQ])
            den = sb("s2_den", [P, NQ])
            rden = sb("s2_rden", [P, NQ])
            probs = sb("s2_probs", [P, 2, GRP, KEYS])
            pT_hi = sb("s2_pT_hi", [P, 2, 512], F32R)
            pT_lo = sb("s2_pT_lo", [P, 2, 512], F32R)
            o_sb = sb("s2_o_sb", [HD, 2, 512])
            s_ps = ps("s2_s_ps", [P, 2, 1024])
            pT_ps = ps("s2_pT_ps", [P, 2, 512])
            o_ps = ps("s2_o_ps", [P, 2, 512])
            fixed_loaded = sem("s2_fixed_loaded")
            mask_ready = sem("s2_mask_ready")
            qk_loaded = [sem(f"s2_qk_loaded{i}") for i in range(2)]
            v_loaded = [sem(f"s2_v_loaded{i}") for i in range(2)]
            s_ready = sem("s2_s_ready")
            max_ready = sem("s2_max_ready")
            neg_ready = sem("s2_neg_ready")
            p_ready = sem("s2_p_ready")
            norm_step = sem("s2_norm_step")
            p_scaled = sem("s2_p_scaled")
            pT_ready = sem("s2_pT_ready")
            hi_ready = sem("s2_hi_ready")
            lo_ready = sem("s2_lo_ready")
            pv_ready = sem("s2_pv_ready")
            o_ready = sem("s2_o_ready")
            o_stored = [sem(f"s2_o_stored{i}") for i in range(2)]
            block = stage.enter_context(nc.Block())
            KTILES = KEYS // P
            HEAD, TAIL = 2, 2

            @block.sync
            def _(sp):
                def load_qk(b, slot, before):
                    if before >= 2:
                        at_turn(sp, s_ready, (b - 1) * NQ)
                    sp.dma_start(f32v(q_in[:, slot]), qT_d[:, :, bass.ds(b * P + CTX, P)].rearrange("h p t -> p h t")).then_inc(qk_loaded[slot], 16)
                    sp.dma_start(f32v(k_in[:, slot]), kT_d[:, :, bass.ds(b * P + CTX, WIN)].rearrange("h p t -> p h t")).then_inc(qk_loaded[slot], 16)

                def load_v(b, slot, before):
                    if before >= 2:
                        at_turn(sp, pv_ready, (b - 1) * 2 * KTILES)
                    sp.dma_start(f32v(v_in[:, slot]), v_d[bass.ds(b * P + CTX, WIN), :, :].rearrange("(j p) a d -> p j a d", p=P)).then_inc(v_loaded[slot], 16)

                def store(b, g):
                    at_turn(sp, o_ready, 2 * b + g + 1)
                    rows = slice(g * GRP * HD, (g + 1) * GRP * HD)
                    sp.dma_start(aT_d[rows, bass.ds(b * P, P)].rearrange("(i d) t -> d i t", d=HD),
                                 o_sb[:, g, :].rearrange("d (i t) -> d i t", i=GRP)).then_inc(o_stored[g], 16)

                fixed = [(f32v(k_ctx[:]), kT_d[:, :, 0:CTX].rearrange("h p t -> p h t")),
                         (f32v(v_ctx[:]), v_d[0:CTX, :, :].rearrange("(j p) a d -> p j a d", p=P)),
                         (mask_in[:], masks), (sink[:], ap_sink[0:1, :].partition_broadcast(P))]
                load_qk(0, 0, 0)
                for dst, src in fixed:
                    sp.dma_start(dst, src).then_inc(fixed_loaded, 16)

                def body(b, slot, before, after):
                    if after >= 1:
                        load_qk(b + 1, 1 - slot, before + 1)
                    load_v(b, slot, before)
                    if before >= 1:
                        store(b - 1, 0)
                        store(b - 1, 1)

                chunks(sp, body, TILES, HEAD, TAIL)
                for g in range(2):
                    store(TILES - 1, g)
                for g in range(2):
                    sp.wait_ge(o_stored[g], 16 * TILES)

            @block.tensor
            def _(pe):
                def scores(b, slot, g, i, variant, heads_before):
                    e = (2 * b + g) * GRP + i
                    h = GRP * g + i
                    if heads_before >= 2:
                        pe.wait_ge(p_ready, e - 1)
                    acc = s_ps[:, i % 2, :]
                    pe.matmul(acc[:, P:512], ident16[:], mask[:, variant, :], start=True, stop=False)
                    for part, stop in ((0, False), (1, True)):
                        pe.matmul(acc[:, P:512], q_in[:, slot, h, :], k_in[:, slot, NKV * part + g, :], start=False, stop=stop)
                    for part in range(2):
                        ins = pe.matmul(acc[:, 512:512 + CTX], q_in[:, slot, h, :], k_ctx[:, NKV * part + g, :], start=part == 0, stop=part == 1)
                    ins.then_inc(s_ready, 1)

                def transpose_tile(y, g, j, groups_before):
                    t = y * KTILES + j
                    if j == 0:
                        pe.wait_ge(p_scaled, (y + 1) * GRP)
                    if groups_before * KTILES + j >= 2:
                        pe.wait_ge(lo_ready, t - 1)
                    for i in range(GRP):
                        ins = pe.transpose(pT_ps[:, (g + j) % 2, i * P:(i + 1) * P], probs[:, g, i, j * P:(j + 1) * P], ident[:])
                    ins.then_inc(pT_ready, 1)

                def values(b, y, slot, g, j, groups_before):
                    t = y * KTILES + j
                    pe.wait_ge(lo_ready, t + 1)
                    if j == 0 and groups_before >= 2:
                        pe.wait_ge(o_ready, y - 1)
                    if j == 0 and g == 0:
                        pe.wait_ge(v_loaded[slot], 8 * (b + 2 - slot))
                    v = v_in[:, slot, j] if j < 3 else v_ctx[:, j - 3]
                    cols = slice(HD * g, HD * (g + 1))
                    ins = product(pe, o_ps[0:HD, g, :], (v[:, 0, cols], v[:, 1, cols]),
                                  (pT_hi[:, (g + j) % 2, :], pT_lo[:, (g + j) % 2, :]), j == 0, j == KTILES - 1)
                    ins.then_inc(pv_ready, 1)

                def group(b, slot, g, before, variant, new):
                    y = 2 * b + g
                    gb = 2 * before + g
                    b1, slot1 = (b, slot) if g == 1 else (b - 1, 1 - slot)
                    for i in range(GRP):
                        if new:
                            scores(b, slot, g, i, variant, gb * GRP + i)
                        if i == 0 and gb >= 2:
                            values(b - 1, y - 2, 1 - slot, g, KTILES - 1, gb - 2)
                        if gb >= 1:
                            transpose_tile(y - 1, 1 - g, i, gb - 1)
                            if i >= 1:
                                values(b1, y - 1, slot1, 1 - g, i - 1, gb - 1)
                    if gb >= 1:
                        transpose_tile(y - 1, 1 - g, KTILES - 1, gb - 1)
                        values(b1, y - 1, slot1, 1 - g, KTILES - 2, gb - 1)

                pe.wait_ge(mask_ready, 1)
                pe.wait_ge(fixed_loaded, 64)

                def body(b, slot, before, after):
                    variant = 0 if before == 0 else 2 if after == 0 else 1
                    pe.wait_ge(qk_loaded[slot], 16 * (b + 2 - slot))
                    for g in range(2):
                        group(b, slot, g, before, variant, True)

                chunks(pe, body, TILES, HEAD, TAIL)
                group(TILES, 0, 0, TILES, 0, False)
                values(TILES - 1, 2 * TILES - 1, 1, 1, KTILES - 1, 9)

            @block.scalar
            def _(act):
                act.wait_ge(fixed_loaded, 64)

                def exponentials(y, g, i, gb):
                    e = y * GRP + i
                    h = GRP * g + i
                    act.wait_ge(neg_ready, e + 1)
                    if gb >= 2:
                        act.wait_ge(p_scaled, e - 2 * GRP + 1)
                        if i == 0:
                            act.wait_ge(pT_ready, (y - 1) * KTILES)
                    act.activation(p_sink[:, h:h + 1], sink[:, h:h + 1], ACT.Exp, bias=neg_max[:, h:h + 1])
                    act.activation(probs[:, g, i, :], s_ps[:, i % 2, P:P + KEYS], ACT.Exp, scale=SCALE,
                                   bias=neg_max[:, h:h + 1], accum_out=p_sum[:, h:h + 1]).then_inc(p_ready, 1)

                def split_hi(y, g, j, gb):
                    t = y * KTILES + j
                    act.wait_ge(pT_ready, t + 1)
                    if gb * KTILES + j >= 2:
                        act.wait_ge(pv_ready, t - 1)
                    act.activation(pT_hi[:, (g + j) % 2, :], pT_ps[:, (g + j) % 2, :], ACT.Copy).then_inc(hi_ready, 1)

                def evacuate(b, y, g, gb):
                    act.wait_ge(pv_ready, (y + 1) * KTILES)
                    if gb >= 2:
                        act.wait_ge(o_stored[g], 16 * b)
                    act.activation(o_sb[:, g, :], o_ps[0:HD, g, :], ACT.Copy).then_inc(o_ready, 1)

                def group(b, slot, g, before, new):
                    y = 2 * b + g
                    gb = 2 * before + g
                    for i in range(GRP):
                        if new:
                            exponentials(y, g, i, gb)
                        if gb >= 1:
                            split_hi(y - 1, 1 - g, i, gb - 1)
                        if i == 1 and gb >= 2:
                            evacuate(b - 1, y - 2, g, gb - 2)
                    if gb >= 1:
                        split_hi(y - 1, 1 - g, KTILES - 1, gb - 1)

                def body(b, slot, before, after):
                    for g in range(2):
                        group(b, slot, g, before, True)

                chunks(act, body, TILES, HEAD, TAIL)
                group(TILES, 0, 0, TILES, False)
                evacuate(TILES - 1, 2 * TILES - 1, 1, 9)

            @block.vector
            def _(dve):
                dve.wait_ge(fixed_loaded, 64)
                dve.tensor_copy(mask[:], mask_in[:])
                dve.tensor_scalar(neg_sink[:], sink[:], -1.0, None, ALU.mult).then_inc(mask_ready, 1)
                dve.wait_ge(mask_ready, 1)

                def maxima(y, g, i, gb):
                    e = y * GRP + i
                    h = GRP * g + i
                    dve.wait_ge(s_ready, e + 1)
                    dve.tensor_reduce(row_max[:, h:h + 1], s_ps[:, i % 2, P:P + KEYS], AXIS.X, ALU.max).then_inc(max_ready, 1)
                    dve.wait_ge(max_ready, e + 1)
                    if gb >= 2:
                        dve.wait_ge(p_ready, e - 2 * GRP + 1)
                    dve.scalar_tensor_tensor(neg_max[:, h:h + 1], row_max[:, h:h + 1], -SCALE, neg_sink[:, h:h + 1],
                                             ALU.mult, ALU.min).then_inc(neg_ready, 1)

                def normalise(y, g, i, gb):
                    e = y * GRP + i
                    h = GRP * g + i
                    dve.wait_ge(p_ready, e + 1)
                    dve.tensor_tensor(den[:, h:h + 1], p_sum[:, h:h + 1], p_sink[:, h:h + 1], ALU.add).then_inc(norm_step, 1)
                    dve.wait_ge(norm_step, 2 * e + 1)
                    dve.reciprocal(rden[:, h:h + 1], den[:, h:h + 1]).then_inc(norm_step, 1)
                    dve.wait_ge(norm_step, 2 * e + 2)
                    dve.tensor_scalar(probs[:, g, i, :], probs[:, g, i, :], rden[:, h:h + 1], None, ALU.mult).then_inc(p_scaled, 1)

                def split_lo(y, g, j, gb):
                    t = y * KTILES + j
                    dve.wait_ge(hi_ready, t + 1)
                    dve.tensor_tensor(pT_lo[:, (g + j) % 2, :], pT_ps[:, (g + j) % 2, :], f32v(pT_hi[:, (g + j) % 2, :]), ALU.subtract).then_inc(lo_ready, 1)

                def group(b, slot, g, before, new):
                    y = 2 * b + g
                    gb = 2 * before + g
                    for i in range(GRP):
                        if new:
                            maxima(y, g, i, gb)
                        if i == 0 and gb >= 1:
                            normalise(y - 1, 1 - g, GRP - 1, gb - 1)
                        if i == 0 and gb >= 2:
                            split_lo(y - 2, g, KTILES - 1, gb - 2)
                        if i >= 1 and gb >= 1:
                            split_lo(y - 1, 1 - g, i - 1, gb - 1)
                        if i >= 1 and new:
                            normalise(y, g, i - 1, gb)
                    if gb >= 1:
                        split_lo(y - 1, 1 - g, KTILES - 2, gb - 1)

                def body(b, slot, before, after):
                    for g in range(2):
                        group(b, slot, g, before, True)

                chunks(dve, body, TILES, HEAD, TAIL)
                group(TILES, 0, 0, TILES, False)
                split_lo(2 * TILES - 1, 1, KTILES - 1, 9)

        NT3 = 12
        BANKS3 = 6

        STEPS = 2 * CONV_K

        def conv_order(half, before):
            if before < 3:
                if half == 0:
                    return None
                return (0, ((2, 3), (0, 1), (2, 3))[before], ((2, 3, 3)[before] * 2 - before) * CW)
            return (half, (0, 1), -3 * CW) if before % 2 else (half, (2, 3), -4 * CW)

        class ConvTaps:

            def __init__(self, name, stage, off):
                sb = lambda n, s: stage.enter_context(nc.sbuf_tensor(name + n, s, F32))
                sem = lambda n: new_sem(stage, name + n)
                self.off = off
                self.w = sb("cw", [P, KT, CONV_K])
                self.b = sb("cb", [P, KT])
                self.u = sb("cu", [P, 2, 2, PAIR + 2 * HALO])
                self.acc = sb("cacc", [P, 2, 2, PAIR])
                self.w_loaded = sem("cw_loaded")
                self.u_loaded = [sem(f"cu_loaded{i}") for i in range(2)]
                self.step = sem("conv_step")
                self.stored = [sem(f"conv_stored{i}") for i in range(2)]

            def load_weights(self, q):
                for t in range(KT):
                    q.dma_start(self.w[:, t, :], cv_dw_w[0, :, t * P:(t + 1) * P].rearrange("k p -> p k"),
                                allow_slow_non_contiguous=True).then_inc(self.w_loaded, 16)
                q.dma_start(self.b[:], cv_dw_b[0, :].rearrange("(t p) -> p t", p=P), allow_slow_non_contiguous=True).then_inc(self.w_loaded, 16)

            def load(self, q, n, slot, before, item, u_stored):
                o, set_, (half, tiles, at) = n - self.off, (slot + self.off) % 2, item
                if before - self.off >= 2:
                    at_turn(q, self.step, (o - 1) * STEPS)
                if u_stored is not None:
                    for i in range(2):
                        at_turn(q, u_stored[i], 32 * n)
                for i, t in enumerate(tiles):
                    rows = slice((4 * half + t) * P, (4 * half + t + 1) * P)
                    q.dma_start(self.u[:, set_, i, :], cuT_d[rows, bass.ds(n * CW + at, PAIR + 2 * HALO)]).then_inc(self.u_loaded[set_], 16)

            def run(self, dve, n, slot, before, item, quarter):
                o, set_, (half, tiles, at) = n - self.off, (slot + self.off) % 2, item
                if quarter == 0:
                    dve.wait_ge(self.w_loaded, 16 * (KT + 1))
                    dve.wait_ge(self.u_loaded[set_], 16 * (o + 2 - set_))
                    if before - self.off >= 2:
                        dve.wait_ge(self.stored[set_], 16 * (o - set_))
                bounds = (0, 7, 15, 23, CONV_K)
                for tap in range(bounds[quarter], bounds[quarter + 1]):
                    for i, t in enumerate(tiles):
                        ch = 4 * half + t
                        acc = self.acc[:, set_, i, :]
                        u = self.u[:, set_, i, tap:tap + PAIR]
                        w = self.w[:, ch, tap:tap + 1]
                        if tap == 0:
                            dve.tensor_scalar(acc, u, w, self.b[:, ch:ch + 1], ALU.mult, ALU.add).then_inc(self.step, 1)
                        else:
                            dve.wait_ge(self.step, o * STEPS + 2 * tap + i - 1)
                            dve.scalar_tensor_tensor(acc, u, w, acc, ALU.mult, ALU.add).then_inc(self.step, 1)

            def store(self, q, n, slot, item):
                o, set_, (half, tiles, at) = n - self.off, (slot + self.off) % 2, item
                at_turn(q, self.step, (o + 1) * STEPS)
                for i, t in enumerate(tiles):
                    rows = slice((4 * half + t) * P, (4 * half + t + 1) * P)
                    q.dma_start(ccT_d[rows, bass.ds(n * CW + at, PAIR)], self.acc[:, set_, i, :]).then_inc(self.stored[set_], 16)

            def finish(self, q, items):
                for set_ in range(2):
                    q.wait_ge(self.stored[set_], 32 * ((items + 1 - set_) // 2))

        def project(name, x_rows, rstd, which, pieces, half):
            conv = half is not None
            with ExitStack() as stage:
                sb = lambda n, s, d=F32: stage.enter_context(nc.sbuf_tensor(name + n, s, d))
                ps = lambda n, s, d=F32: stage.enter_context(nc.psum_tensor(name + n, s, d))
                sem = lambda n: new_sem(stage, name + n)
                w_hi = sb("w_hi", [P, KT, NT3 * P], F32R)
                w_lo = sb("w_lo", [P, KT, NT3 * P], F32R)
                split_weights(name + "w", pieces, w_hi, w_lo)
                xin = sb("x", [P, TPC, D])
                xT = sb("xT", [P, KT, CW])
                xT_hi = sb("xT_hi", [P, KT, CW], F32R)
                xT_lo = sb("xT_lo", [P, KT, CW], F32R)
                sig = sb("sig", [P, 2, CW]) if conv else None
                u_sb = sb("u_sb", [P, 2, CW])
                g_sb = sb("g_sb", [P, 2, CW])
                tr_ps = ps("tr_ps", [P, 2, CW])
                out_ps = ps("out_ps", [P, BANKS3, CW])
                x_loaded = [sem(f"x_loaded{s}") for s in range(TPC)]
                xn_ready = sem("xn_ready")
                tr_ready = sem("tr_ready")
                xT_ready = sem("xT_ready")
                hi_ready = sem("hi_ready")
                lo_ready = sem("lo_ready")
                x_used = sem("x_used")
                out_ready = sem("out_ready")
                act_done = sem("act_done")
                u_done = sem("u_done")
                u_stored = [sem(f"u_stored{i}") for i in range(2)]
                g_stored = [sem(f"g_stored{i}") for i in range(2)]
                if conv:
                    taps = ConvTaps(name, stage, 3 if half == 0 else 0)
                block = stage.enter_context(nc.Block())
                if conv:
                    kinds = ["b", "a", "g"] * 4
                    w_at = [(4 if k == "b" else 0 if k == "a" else 8) + t // 3 for t, k in enumerate(kinds)]
                else:
                    kinds = ["u"] * 4 + ["g"] * 8
                    w_at = list(range(NT3))
                acts = [k != "a" for k in kinds]
                act_n = sum(acts)
                act_no = [sum(acts[:t]) for t in range(NT3)]
                HEAD, TAIL = (3, 1) if conv else (2, 2)

                def freed(eng, n, t, before):
                    if before * NT3 + t < BANKS3:
                        return
                    back, t0 = (0, t - BANKS3) if t >= BANKS3 else (1, t - BANKS3 + NT3)
                    if acts[t0]:
                        eng.wait_ge(act_done, (n - back) * act_n + act_no[t0] + 1)
                    else:
                        eng.wait_ge(u_done, (n - back) * 4 + t0 // 3 + 1)

                @block.sync
                def _(sp):
                    def load(n, before):
                        if before >= 1:
                            at_turn(sp, tr_ready, n * KT)
                        for s in range(TPC):
                            sp.dma_start(xin[:, s, :], x_rows[bass.ds(n * CW + s * P, P), :]).then_inc(x_loaded[s], 16)

                    def body(n, slot, before, after):
                        if before == 0:
                            load(0, 0)
                        if after >= 1:
                            load(n + 1, before + 1)
                        u_no = g_no = 0
                        cols = bass.ds(n * CW, CW)
                        for t in range(NT3):
                            if kinds[t] in "ua":
                                u_no += 1
                                if conv:
                                    at_turn(sp, u_done, n * 4 + u_no)
                                    dst = cuT_d[(4 * half + u_no - 1) * P:(4 * half + u_no) * P, bass.ds(n * CW + HALO, CW)]
                                else:
                                    at_turn(sp, act_done, n * act_n + act_no[t] + 1)
                                    dst = uT_d[(u_no - 1) * P:u_no * P, bass.ds(n * CW + PHALO, CW)]
                                i = (u_no - 1) % 2
                                sp.dma_start(dst, u_sb[:, i, :]).then_inc(u_stored[i], 16)
                            elif kinds[t] == "g":
                                g_no += 1
                                at_turn(sp, act_done, n * act_n + act_no[t] + 1)
                                if conv:
                                    dst = cgT_d[(4 * half + g_no - 1) * P:(4 * half + g_no) * P, cols]
                                else:
                                    dst = gT_d[(g_no - 1) * P:g_no * P, cols]
                                i = (g_no - 1) % 2
                                sp.dma_start(dst, g_sb[:, i, :]).then_inc(g_stored[i], 16)

                    chunks(sp, body, NCH, HEAD, TAIL)
                    for i in range(2):
                        sp.wait_ge(u_stored[i], 16 * NCH * 2)
                        sp.wait_ge(g_stored[i], 16 * NCH * (2 if conv else 4))

                @block.tensor
                def _(pe):
                    def transpose_x(n, k, before):
                        if k == 0:
                            pe.wait_ge(xn_ready, n + 1)
                        if before * KT + k >= 2:
                            pe.wait_ge(xT_ready, n * KT + k - 1)
                        for s in range(TPC):
                            ins = pe.transpose(tr_ps[:, k % 2, s * P:(s + 1) * P], xin[:, s, k * P:(k + 1) * P], ident[:])
                        ins.then_inc(tr_ready, 1)

                    def body(n, slot, before, after):
                        if before == 0:
                            for k in range(KT):
                                transpose_x(0, k, 0)
                        for t in range(NT3):
                            freed(pe, n, t, before)
                            cols = slice(w_at[t] * P, (w_at[t] + 1) * P)
                            for k in range(KT):
                                if t == 0:
                                    pe.wait_ge(lo_ready, n * KT + k + 1)
                                ins = product(pe, out_ps[:, t % BANKS3, :], (w_hi[:, k, cols], w_lo[:, k, cols]),
                                              (xT_hi[:, k, :], xT_lo[:, k, :]), k == 0, k == KT - 1)
                                if t == NT3 - 1:
                                    ins.then_inc(x_used, 1)
                                elif k == KT - 1:
                                    ins.then_inc(out_ready, 1)
                            if after >= 1 and 3 <= t < 3 + KT:
                                transpose_x(n + 1, t - 3, before + 1)

                    chunks(pe, body, NCH, HEAD, TAIL)

                def tile_ready(eng, n, t):
                    if t == NT3 - 1:
                        eng.wait_ge(x_used, (n + 1) * KT)
                    else:
                        eng.wait_ge(out_ready, n * (NT3 - 1) + t + 1)

                @block.scalar
                def _(act):
                    def evacuate_xT(n, k, before):
                        act.wait_ge(tr_ready, n * KT + k + 1)
                        if before >= 1:
                            act.wait_ge(lo_ready, (n - 1) * KT + k + 1)
                        act.activation(xT[:, k, :], tr_ps[:, k % 2, :], ACT.Identity,
                                       scale=G[:, which, k:k + 1], bias=S[:, which, k:k + 1]).then_inc(xT_ready, 1)

                    def split_hi(n, k, before):
                        act.wait_ge(xT_ready, n * KT + k + 1)
                        if before >= 1:
                            act.wait_ge(x_used, (n - 1) * KT + k + 1)
                        act.activation(xT_hi[:, k, :], xT[:, k, :], ACT.Copy).then_inc(hi_ready, 1)

                    def evacuate(n, t, before):
                        bank = out_ps[:, t % BANKS3, :]
                        tile_ready(act, n, t)
                        no = kinds[:t].count(kinds[t])
                        if kinds[t] == "b":
                            if before * 4 + no >= 2:
                                act.wait_ge(u_done, n * 4 + no - 1)
                            act.activation(sig[:, no % 2, :], bank, ACT.Sigmoid).then_inc(act_done, 1)
                        else:
                            per = kinds.count(kinds[t])
                            dst, stored = (u_sb, u_stored) if kinds[t] == "u" else (g_sb, g_stored)
                            if before * per + no >= 2:
                                act.wait_ge(stored[no % 2], 8 * (n * per + no - no % 2))
                            func = ACT.Silu if kinds[t] == "g" and not conv else ACT.Copy
                            act.activation(dst[:, no % 2, :], bank, func).then_inc(act_done, 1)

                    def body(n, slot, before, after):
                        if before == 0:
                            for k in range(KT):
                                evacuate_xT(0, k, 0)
                                split_hi(0, k, 0)
                        for t in range(NT3):
                            if t == NT3 - 1 and after >= 1:
                                for k in range(KT):
                                    split_hi(n + 1, k, before + 1)
                            if acts[t]:
                                evacuate(n, t, before)
                            if after >= 1 and 3 <= t < 3 + KT:
                                evacuate_xT(n + 1, t - 3, before + 1)

                    chunks(act, body, NCH, HEAD, TAIL)

                @block.vector
                def _(dve):
                    def scale_x(n, before):
                        for s in range(TPC):
                            dve.wait_ge(x_loaded[s], 16 * (n + 1))
                            ins = dve.tensor_scalar(xin[:, s, :], xin[:, s, :], rstd[:, bass.ds(n * TPC + s, 1)], None, ALU.mult)
                        ins.then_inc(xn_ready, 1)

                    def split_lo(n, k):
                        dve.wait_ge(hi_ready, n * KT + k + 1)
                        dve.tensor_tensor(xT_lo[:, k, :], xT[:, k, :], f32v(xT_hi[:, k, :]), ALU.subtract).then_inc(lo_ready, 1)

                    def gated(n, j, before):
                        dve.wait_ge(out_ready, n * (NT3 - 1) + 3 * j + 2)
                        dve.wait_ge(act_done, n * act_n + act_no[3 * j] + 1)
                        if before * 4 + j >= 2:
                            dve.wait_ge(u_stored[j % 2], 8 * (n * 4 + j - j % 2))
                        dve.tensor_tensor(u_sb[:, j % 2, :], out_ps[:, (3 * j + 1) % BANKS3, :], sig[:, j % 2, :], ALU.mult).then_inc(u_done, 1)

                    def body(n, slot, before, after):
                        if before == 0:
                            scale_x(0, 0)
                            for k in range(KT):
                                split_lo(0, k)
                        if after >= 1:
                            scale_x(n + 1, before + 1)
                        if conv:
                            item = conv_order(half, before)
                            for j in range(4):
                                if item is not None:
                                    taps.run(dve, n, slot, before, item, j)
                                gated(n, j, before)
                        if after >= 1:
                            for k in range(KT):
                                split_lo(n + 1, k)

                    chunks(dve, body, NCH, HEAD, TAIL)

                @block.gpsimd
                def _(pool):
                    if not conv:
                        return
                    taps.load_weights(pool)

                    def body(n, slot, before, after):
                        item = conv_order(half, before)
                        if item is not None:
                            taps.load(pool, n, slot, before, item, u_stored if item[0] == half else None)
                            taps.store(pool, n, slot, item)

                    chunks(pool, body, NCH, HEAD, TAIL)
                    taps.finish(pool, NCH - (3 if half == 0 else 0))


        project("s3_", x[0], rstd0[:, CTX // P:], 0, [(0, lambda k: ap_w_in[0, k * P:(k + 1) * P, QKV:QKV + NT3 * P], NT3 * P)], None)

        clear_semaphores()
        def load_out_weights(name, w_out, which, stage):
            w_hi = stage.enter_context(nc.sbuf_tensor(name + "w_hi", [P, KT, D], F32R))
            w_lo = stage.enter_context(nc.sbuf_tensor(name + "w_lo", [P, KT, D], F32R))
            with ExitStack() as inner:
                row = inner.enter_context(nc.sbuf_tensor(name + "gate", [P, D], F32))
                row_loaded = new_sem(inner, name + "gate_loaded")
                split_weights(name + "w", [(0, lambda k: w_out[0, k * P:(k + 1) * P, :], D)], w_hi, w_lo,
                              (row, row_loaded, gate_d[which:which + 1, :].partition_broadcast(P)))
            return w_hi, w_lo

        def out_product(pe, acc, y_hi, y_lo, w_hi, w_lo, s, k):
            ts = slice(s * P, (s + 1) * P)
            for h in range(2):
                cols = slice(512 * h, 512 * (h + 1))
                ins = product(pe, acc[:, h, :], (y_hi[:, k, ts], y_lo[:, k, ts]),
                              (w_hi[:, k, cols], w_lo[:, k, cols]), k == 0, k == KT - 1)
            return ins

        with ExitStack() as stage:
            sb = lambda n, s, d=F32: stage.enter_context(nc.sbuf_tensor("s4_" + n, s, d))
            ps = lambda n, s, d=F32: stage.enter_context(nc.psum_tensor("s4_" + n, s, d))
            sem = lambda n: new_sem(stage, "s4_" + n)
            NG = len(POOL_WINDOWS)
            UW = CW + 2 * PHALO
            w_hi, w_lo = load_out_weights("s4_", ap_w_out, 0, stage)
            pw_hi = sb("pw_hi", [P, NG, P], F32R)
            pw_lo = sb("pw_lo", [P, NG, P], F32R)
            split_weights("s4_pw", [(0, lambda k: ap_pool_w[0, k, :, :], P)], pw_hi, pw_lo)
            pscale = sb("pscale", [P, NG])
            a_in = sb("a_in", [P, NG, CW])
            y = sb("y", [P, 2, KT, CW])
            u_in = sb("u_in", [P, NG, UW])
            cnt = sb("cnt", [P, NG, CW])
            sums = sb("sums", [P, 2, UW])
            d = sb("d", [P, 2, CW])
            d_hi = sb("d_hi", [P, 2, CW], F32R)
            d_lo = sb("d_lo", [P, 2, CW], F32R)
            y_hi = sb("y_hi", [P, KT, CW], F32R)
            y_lo = sb("y_lo", [P, KT, CW], F32R)
            xr = sb("xr", [P, TPC, D])
            junk = sb("junk", [P, D])
            ss1 = sb("ss1", [P, TILES])
            tmp1 = sb("tmp1", [P, TILES])
            out_ps = ps("out_ps", [P, 2, 2, 512])
            pool_ps = ps("pool_ps", [P, NG, 512])
            pscale_loaded = sem("pscale_loaded")
            in_loaded = sem("in_loaded")
            g_loaded = [sem(f"g_loaded{i}") for i in range(2)]
            xr_loaded = [sem(f"xr_loaded{i}") for i in range(TPC)]
            sum_step = sem("sum_step")
            d_ready = sem("d_ready")
            d_hi_ready = sem("d_hi_ready")
            d_lo_ready = sem("d_lo_ready")
            pool_ready = sem("pool_ready")
            y_ready = sem("y_ready")
            hi_ready = sem("hi_ready")
            lo_ready = sem("lo_ready")
            y_used = sem("y_used")
            out_ready = sem("out_ready")
            x1_ready = sem("x1_ready")
            ss_ready = sem("ss_ready")
            x1_stored = [sem(f"x1_stored{i}") for i in range(TPC)]
            fin_step = sem("fin_step")
            block = stage.enter_context(nc.Block())
            HEAD, TAIL = 2, 2
            SUM_STEPS = sum(len(bin(w)) - 3 for w in POOL_WINDOWS) + NG

            @block.sync
            def _(sp):
                sp.dma_start(pscale[:], ap_pool_scale[0, :].rearrange("(g p) -> p g", p=P), allow_slow_non_contiguous=True).then_inc(pscale_loaded, 16)

                def load_in(n, slot, before):
                    cols = bass.ds(n * CW, CW)
                    if before >= 2:
                        at_turn(sp, lo_ready, (n - 1) * KT)
                    sp.dma_start(y[:, slot], gT_d[:, cols].rearrange("(k p) t -> p k t", p=P)).then_inc(g_loaded[slot], 16)
                    if before >= 1:
                        at_turn(sp, y_ready, n * KT)
                    sp.dma_start(a_in[:], aT_d[:, cols].rearrange("(k p) t -> p k t", p=P)).then_inc(in_loaded, 16)
                    sp.dma_start(u_in[:], uT_d[:, bass.ds(n * CW, UW)].rearrange("(k p) t -> p k t", p=P)).then_inc(in_loaded, 16)
                    sp.dma_start(cnt[:], counts[:, cols].partition_broadcast(P)).then_inc(in_loaded, 16)

                def load_x(n, s, before):
                    if before >= 1:
                        at_turn(sp, x1_stored[s], 16 * n)
                        at_turn(sp, ss_ready, (n - 1) * TPC + s + 1)
                    sp.dma_start(xr[:, s, :], x[0, bass.ds(n * CW + s * P, P), :]).then_inc(xr_loaded[s], 16)

                def body(n, slot, before, after):
                    if before == 0:
                        load_in(0, 0, 0)
                        for s in range(TPC):
                            load_x(0, s, 0)
                        load_in(1, 1, 1)
                    for s in range(TPC):
                        at_turn(sp, x1_ready, n * TPC + s + 1)
                        sp.dma_start(x1_d[bass.ds(n * CW + s * P, P), :], xr[:, s, :]).then_inc(x1_stored[s], 16)
                    if after >= 2:
                        load_in(n + 2, slot, before + 2)
                    if after >= 1:
                        for s in range(TPC):
                            load_x(n + 1, s, before + 1)

                chunks(sp, body, NCH, HEAD, TAIL)
                for s in range(TPC):
                    sp.wait_ge(x1_stored[s], 16 * NCH)

            @block.tensor
            def _(pe):
                def pool_product(n, g, before):
                    pe.wait_ge(d_lo_ready, n * NG + g + 1)
                    if before >= 1:
                        pe.wait_ge(y_ready, (n - 1) * KT + NG + g + 1)
                    product(pe, pool_ps[:, g, :], (pw_hi[:, g, :], pw_lo[:, g, :]),
                            (d_hi[:, g % 2, :], d_lo[:, g % 2, :]), True, True).then_inc(pool_ready, 1)

                def body(n, slot, before, after):
                    if before == 0:
                        for g in range(NG):
                            pool_product(0, g, 0)
                    for s in range(TPC):
                        if before * TPC + s >= 2:
                            pe.wait_ge(x1_ready, n * TPC + s - 1)
                        for k in range(KT):
                            if s == 0:
                                pe.wait_ge(lo_ready, n * KT + k + 1)
                            ins = out_product(pe, out_ps[:, s % 2], y_hi, y_lo, w_hi, w_lo, s, k)
                            if s == TPC - 1:
                                ins.then_inc(y_used, 1)
                            elif k == KT - 1:
                                ins.then_inc(out_ready, 1)
                        if after >= 1 and s < 2:
                            for g in (2 * s, 2 * s + 1):
                                pool_product(n + 1, g, before + 1)

                chunks(pe, body, NCH, HEAD, TAIL)

            @block.scalar
            def _(act):
                def split_d(n, g, before):
                    act.wait_ge(d_ready, n * NG + g + 1)
                    if before * NG + g >= 2:
                        act.wait_ge(pool_ready, n * NG + g - 1)
                    act.activation(d_hi[:, g % 2, :], d[:, g % 2, :], ACT.Copy).then_inc(d_hi_ready, 1)

                def split_y(n, slot, k, before):
                    act.wait_ge(y_ready, n * KT + k + 1)
                    if before >= 1:
                        act.wait_ge(y_used, (n - 1) * KT + k + 1)
                    act.activation(y_hi[:, k, :], y[:, slot, k, :], ACT.Copy).then_inc(hi_ready, 1)

                def squares(n, s, before):
                    act.wait_ge(x1_ready, n * TPC + s + 1)
                    if before * TPC + s >= 1:
                        act.wait_ge(ss_ready, n * TPC + s)
                    act.activation(junk[:], xr[:, s, :], ACT.Square, accum_out=ss1[:, bass.ds(n * TPC + s, 1)]).then_inc(ss_ready, 1)

                def body(n, slot, before, after):
                    if before == 0:
                        for g in range(NG):
                            split_d(0, g, 0)
                        for k in range(KT):
                            split_y(0, 0, k, 0)
                    for s in range(TPC):
                        if after >= 1 and s < 2:
                            split_d(n + 1, 2 * s, before + 1)
                            split_d(n + 1, 2 * s + 1, before + 1)
                        if after >= 1 and s == TPC - 1:
                            for k in range(KT):
                                split_y(n + 1, 1 - slot, k, before + 1)
                        squares(n, s, before)

                chunks(act, body, NCH, HEAD, TAIL)

            @block.vector
            def _(dve):
                def gate_attention(n, slot, k):
                    if k == 0:
                        dve.wait_ge(g_loaded[slot], 8 * (n + 2 - slot))
                    dve.tensor_tensor(y[:, slot, k, :], y[:, slot, k, :], a_in[:, k, :], ALU.mult).then_inc(y_ready, 1)

                def pool_mean(n, g, before):
                    step = n * SUM_STEPS + sum(len(bin(w)) - 3 for w in POOL_WINDOWS[:g]) + g
                    w = POOL_WINDOWS[g]
                    at = PHALO - w // 2
                    if g == 0:
                        dve.wait_ge(in_loaded, 48 * (n + 1))
                    if before * NG + g >= 1:
                        dve.wait_ge(d_ready, n * NG + g)
                    src, width = u_in[:, g, :], 1
                    while width < w:
                        length = CW + w - 2 * width
                        dst = sums[:, (width.bit_length() - 1) % 2, :]
                        dve.tensor_tensor(dst[:, at:at + length], src[:, at:at + length], src[:, at + width:at + width + length], ALU.add).then_inc(sum_step, 1)
                        step = step + 1
                        dve.wait_ge(sum_step, step)
                        src, width = dst, 2 * width
                    dve.tensor_tensor(src[:, at:at + CW], src[:, at:at + CW], cnt[:, g, :], ALU.mult).then_inc(sum_step, 1)
                    dve.wait_ge(sum_step, step + 1)
                    if before * NG + g >= 2:
                        dve.wait_ge(d_lo_ready, n * NG + g - 1)
                    dve.tensor_tensor(d[:, g % 2, :], src[:, at:at + CW], u_in[:, g, PHALO:PHALO + CW], ALU.subtract).then_inc(d_ready, 1)

                def split_d(n, g, before):
                    dve.wait_ge(d_hi_ready, n * NG + g + 1)
                    if before * NG + g >= 2:
                        dve.wait_ge(pool_ready, n * NG + g - 1)
                    dve.tensor_tensor(d_lo[:, g % 2, :], d[:, g % 2, :], f32v(d_hi[:, g % 2, :]), ALU.subtract).then_inc(d_lo_ready, 1)

                def gate_pool(n, slot, g):
                    dve.wait_ge(pool_ready, n * NG + g + 1)
                    dve.scalar_tensor_tensor(y[:, slot, NG + g, :], pool_ps[:, g, :], pscale[:, g:g + 1], y[:, slot, NG + g, :],
                                             ALU.mult, ALU.mult).then_inc(y_ready, 1)

                def split_y(n, slot, k):
                    dve.wait_ge(hi_ready, n * KT + k + 1)
                    dve.tensor_tensor(y_lo[:, k, :], y[:, slot, k, :], f32v(y_hi[:, k, :]), ALU.subtract).then_inc(lo_ready, 1)

                def residual(n, s):
                    if s == TPC - 1:
                        dve.wait_ge(y_used, (n + 1) * KT)
                    else:
                        dve.wait_ge(out_ready, n * (TPC - 1) + s + 1)
                    dve.wait_ge(xr_loaded[s], 16 * (n + 1))
                    dve.tensor_tensor(xr[:, s, :], xr[:, s, :], out_ps[:, s % 2].rearrange("p h c -> p (h c)"), ALU.add).then_inc(x1_ready, 1)

                dve.wait_ge(pscale_loaded, 16)

                def prepare(n, slot, before, part):
                    if part == 0:
                        for g in range(NG):
                            pool_mean(n, g, before)
                            gate_attention(n, slot, g)
                            split_d(n, g, before)
                    elif part == 1:
                        for g in range(NG):
                            gate_pool(n, slot, g)
                    else:
                        for k in range(KT):
                            split_y(n, slot, k)

                def body(n, slot, before, after):
                    if before == 0:
                        for part in range(3):
                            prepare(0, 0, 0, part)
                    if after >= 1:
                        pool_mean(n + 1, 0, before + 1)
                        gate_attention(n + 1, 1 - slot, 0)
                        split_d(n + 1, 0, before + 1)
                        pool_mean(n + 1, 1, before + 1)
                        gate_attention(n + 1, 1 - slot, 1)
                        split_d(n + 1, 1, before + 1)
                    residual(n, 0)
                    if after >= 1:
                        pool_mean(n + 1, 2, before + 1)
                        gate_attention(n + 1, 1 - slot, 2)
                        split_d(n + 1, 2, before + 1)
                        pool_mean(n + 1, 3, before + 1)
                        gate_attention(n + 1, 1 - slot, 3)
                        split_d(n + 1, 3, before + 1)
                    residual(n, 1)
                    if after >= 1:
                        prepare(n + 1, 1 - slot, before + 1, 1)
                    residual(n, 2)
                    if after >= 1:
                        prepare(n + 1, 1 - slot, before + 1, 2)
                    residual(n, 3)

                chunks(dve, body, NCH, HEAD, TAIL)
                dve.wait_ge(ss_ready, TILES)
                dve.tensor_scalar(ss1[:], ss1[:], 1.0 / D, EPS, ALU.mult, ALU.add).then_inc(fin_step, 1)
                dve.wait_ge(fin_step, 1)
                rsqrt(dve, fin_step, 1, rstd1[:], ss1[:], tmp1[:])

        clear_semaphores()
        for half in range(2):
            if half == 1:
                clear_semaphores()
            cols = lambda k, part, half=half: cv_w_in[0, k * P:(k + 1) * P, part * D + half * 512:part * D + half * 512 + 512]
            project(f"s5{'ab'[half]}_", x1_d, rstd1[:, :], 2,
                    [(512 * part, lambda k, part=part: cols(k, part), 512) for part in range(3)], half)

        clear_semaphores()
        with ExitStack() as stage:
            taps = ConvTaps("s5c_", stage, 0)
            items = [(1,) + conv_order(1, n)[1:] for n in range(3)]
            block = stage.enter_context(nc.Block())

            @block.sync
            def _(sp):
                taps.load_weights(sp)
                for n, item in enumerate(items):
                    taps.load(sp, n, n % 2, n, item, None)
                for n, item in enumerate(items):
                    taps.store(sp, n, n % 2, item)
                taps.finish(sp, 3)

            @block.vector
            def _(dve):
                for n, item in enumerate(items):
                    for quarter in range(4):
                        taps.run(dve, n, n % 2, n, item, quarter)

        clear_semaphores()
        with ExitStack() as stage:
            sb = lambda n, s, d=F32: stage.enter_context(nc.sbuf_tensor("s6_" + n, s, d))
            ps = lambda n, s, d=F32: stage.enter_context(nc.psum_tensor("s6_" + n, s, d))
            sem = lambda n: new_sem(stage, "s6_" + n)
            w_hi, w_lo = load_out_weights("s6_", cv_w_out, 1, stage)
            averager = sb("averager", [P, P])
            ln_g = sb("ln_g", [P, KT])
            ln_b = sb("ln_b", [P, KT])
            norm_g = sb("norm_g", [P, D])
            z = sb("z", [P, 2, KT, CW])
            y = sb("y", [P, KT, CW])
            ch_sum = sb("ch_sum", [P, CW])
            sq = sb("sq", [P, 2, CW])
            sq_sum = sb("sq_sum", [P, CW])
            ln_var = sb("ln_var", [P, CW])
            ln_rstd = sb("ln_rstd", [P, CW])
            ln_tmp = sb("ln_tmp", [P, CW])
            y_hi = sb("y_hi", [P, KT, CW], F32R)
            y_lo = sb("y_lo", [P, KT, CW], F32R)
            xr = sb("xr", [P, 2, TPC, D])
            junk = sb("junk", [P, D])
            ss = sb("ss", [P, TPC])
            fin_var = sb("fin_var", [P, TPC])
            fin_rstd = sb("fin_rstd", [P, TPC])
            fin_tmp = sb("fin_tmp", [P, TPC])
            out_ps = ps("out_ps", [P, 2, 2, 512])
            mean_ps = ps("mean_ps", [P, CW])
            var_ps = ps("var_ps", [P, CW])
            fixed_loaded = sem("fixed_loaded")
            averager_made = sem("averager_made")
            z_loaded = [sem(f"z_loaded{i}") for i in range(2)]
            g_loaded = sem("g_loaded")
            xr_loaded = [sem(f"xr_loaded{i}") for i in range(2)]
            sum_step = sem("sum_step")
            mean_ready = sem("mean_ready")
            centred = sem("centred")
            sq_ready = sem("sq_ready")
            sq_step = sem("sq_step")
            var_ready = sem("var_ready")
            rs_step = sem("rs_step")
            z_ready = sem("z_ready")
            sg_ready = sem("sg_ready")
            ln_ready = sem("ln_ready")
            y_ready = sem("y_ready")
            hi_ready = sem("hi_ready")
            lo_ready = sem("lo_ready")
            y_used = sem("y_used")
            out_ready = sem("out_ready")
            x2_ready = sem("x2_ready")
            ss_ready = sem("ss_ready")
            fin_step = sem("fin_step")
            fin_scaled = sem("fin_scaled")
            o_ready = sem("o_ready")
            o_stored = [sem(f"o_stored{i}") for i in range(2)]
            block = stage.enter_context(nc.Block())
            HEAD, TAIL = 2, 2
            SUMS = KT - 1

            @block.sync
            def _(sp):
                def load_z(n, slot, before):
                    if before >= 2:
                        at_turn(sp, y_ready, (n - 1) * KT)
                    sp.dma_start(z[:, slot], ccT_d[:, bass.ds(n * CW, CW)].rearrange("(k p) t -> p k t", p=P)).then_inc(z_loaded[slot], 16)

                def load_g(n, before):
                    if before >= 1:
                        at_turn(sp, lo_ready, n * KT)
                    sp.dma_start(y[:], cgT_d[:, bass.ds(n * CW, CW)].rearrange("(k p) t -> p k t", p=P)).then_inc(g_loaded, 16)

                def load_x(n, slot, before, s):
                    if before >= 2:
                        at_turn(sp, o_stored[slot], 8 * TPC * (n - slot))
                    sp.dma_start(xr[:, slot, s, :], x1_d[bass.ds(n * CW + s * P, P), :]).then_inc(xr_loaded[slot], 16)

                def store(n, slot):
                    for s in range(TPC):
                        at_turn(sp, o_ready, n * TPC + s + 1)
                        sp.dma_start(out[0, bass.ds(n * CW + s * P, P), :], xr[:, slot, s, :]).then_inc(o_stored[slot], 16)

                def body(n, slot, before, after):
                    if before == 0:
                        load_z(0, 0, 0)
                        load_g(0, 0)
                        load_z(1, 1, 1)
                        for s in range(TPC):
                            load_x(0, 0, 0, s)
                    if after >= 2:
                        load_z(n + 2, slot, before + 2)
                    if after >= 1:
                        load_g(n + 1, before + 1)
                    if before >= 1:
                        store(n - 1, 1 - slot)
                    if after >= 1:
                        for s in range(TPC):
                            load_x(n + 1, 1 - slot, before + 1, s)

                smalls = [(ln_g[:], cv_ln_g[0, :].rearrange("(k p) -> p k", p=P)), (ln_b[:], cv_ln_b[0, :].rearrange("(k p) -> p k", p=P)),
                          (norm_g[:], final_norm_g.rearrange("(a d) -> a d", a=1).partition_broadcast(P))]
                for dst, src in smalls:
                    sp.dma_start(dst, src, allow_slow_non_contiguous=True).then_inc(fixed_loaded, 16)
                chunks(sp, body, NCH, HEAD, TAIL)
                store(NCH - 1, (NCH - 1) % 2)
                for slot in range(2):
                    sp.wait_ge(o_stored[slot], 16 * TPC * NCH // 2)

            @block.gpsimd
            def _(pool):
                pool.memset(averager[:], 1.0 / D).then_inc(averager_made, 1)
                pool.wait_ge(fixed_loaded, 48)

                def channel_sums(n, slot, before):
                    pool.wait_ge(z_loaded[slot], 8 * (n + 2 - slot))
                    if before >= 1:
                        pool.wait_ge(mean_ready, n)
                    for k in range(1, KT):
                        if k == 1:
                            ins = pool.tensor_tensor(ch_sum[:], z[:, slot, 0, :], z[:, slot, 1, :], ALU.add)
                        else:
                            pool.wait_ge(sum_step, n * SUMS + k - 1)
                            ins = pool.tensor_tensor(ch_sum[:], ch_sum[:], z[:, slot, k, :], ALU.add)
                        ins.then_inc(sum_step, 1)

                def weigh(n, slot):
                    for s in range(TPC):
                        pool.wait_ge(fin_scaled, n * TPC + s + 1)
                        pool.tensor_tensor(xr[:, slot, s, :], xr[:, slot, s, :], norm_g[:], ALU.mult).then_inc(o_ready, 1)

                def body(n, slot, before, after):
                    if before == 0:
                        channel_sums(0, 0, 0)
                        channel_sums(1, 1, 1)
                    if before >= 1:
                        weigh(n - 1, 1 - slot)
                    if after >= 2:
                        channel_sums(n + 2, slot, before + 2)

                chunks(pool, body, NCH, HEAD, TAIL)
                weigh(NCH - 1, (NCH - 1) % 2)

            @block.tensor
            def _(pe):
                def mean(n, before):
                    pe.wait_ge(sum_step, (n + 1) * SUMS)
                    if before >= 1:
                        pe.wait_ge(centred, n * KT)
                    pe.matmul(mean_ps[:], averager[:], ch_sum[:], start=True, stop=True).then_inc(mean_ready, 1)

                def variance(n, before):
                    pe.wait_ge(sq_step, (n + 1) * SUMS)
                    if before >= 1:
                        pe.wait_ge(rs_step, (n - 1) * (RSQRT_STEPS + 1) + 1)
                    pe.matmul(var_ps[:], averager[:], sq_sum[:], start=True, stop=True).then_inc(var_ready, 1)

                pe.wait_ge(averager_made, 1)

                def body(n, slot, before, after):
                    if before == 0:
                        mean(0, 0)
                        variance(0, 0)
                        mean(1, 1)
                    for s in range(TPC):
                        if before * TPC + s >= 2:
                            pe.wait_ge(x2_ready, n * TPC + s - 1)
                        if after >= 2 and s == TPC - 1:
                            mean(n + 2, before + 2)
                        for k in range(KT):
                            if s == 0:
                                pe.wait_ge(lo_ready, n * KT + k + 1)
                            ins = out_product(pe, out_ps[:, s % 2], y_hi, y_lo, w_hi, w_lo, s, k)
                            if s == TPC - 1:
                                ins.then_inc(y_used, 1)
                            elif k == KT - 1:
                                ins.then_inc(out_ready, 1)
                            if s == 0 and k == 1 and after >= 1:
                                variance(n + 1, before + 1)

                chunks(pe, body, NCH, HEAD, TAIL)

            @block.scalar
            def _(act):
                def square(n, slot, k, before):
                    act.wait_ge(centred, n * KT + k + 1)
                    if before * KT + k >= 2:
                        act.wait_ge(sq_step, n * SUMS + (max(k - 2, 1) if k >= 2 else 0))
                    act.activation(sq[:, k % 2, :], z[:, slot, k, :], ACT.Square).then_inc(sq_ready, 1)

                def silu_gate(n, k):
                    if k == 0:
                        act.wait_ge(g_loaded, 16 * (n + 1))
                    act.activation(y[:, k, :], y[:, k, :], ACT.Silu).then_inc(sg_ready, 1)

                def silu_ln(n, slot, k):
                    act.wait_ge(z_ready, n * KT + k + 1)
                    act.activation(z[:, slot, k, :], z[:, slot, k, :], ACT.Silu, scale=ln_g[:, k:k + 1],
                                   bias=ln_b[:, k:k + 1]).then_inc(ln_ready, 1)

                def split_hi(n, k, before):
                    act.wait_ge(y_ready, n * KT + k + 1)
                    if before >= 1:
                        act.wait_ge(y_used, (n - 1) * KT + k + 1)
                    act.activation(y_hi[:, k, :], y[:, k, :], ACT.Copy).then_inc(hi_ready, 1)

                def squares(n, slot, s, before):
                    act.wait_ge(x2_ready, n * TPC + s + 1)
                    if before * TPC + s >= 1:
                        act.wait_ge(ss_ready, n * TPC + s)
                    if before >= 1 and s == 0:
                        act.wait_ge(fin_step, (n - 1) * (RSQRT_STEPS + 1) + 1)
                    act.activation(junk[:], xr[:, slot, s, :], ACT.Square, accum_out=ss[:, s:s + 1]).then_inc(ss_ready, 1)

                def scale_out(n, slot):
                    act.wait_ge(fin_step, (n + 1) * (RSQRT_STEPS + 1))
                    for s in range(TPC):
                        act.activation(xr[:, slot, s, :], xr[:, slot, s, :], ACT.Copy, scale=fin_rstd[:, s:s + 1]).then_inc(fin_scaled, 1)

                act.wait_ge(fixed_loaded, 48)

                def body(n, slot, before, after):
                    if before == 0:
                        for k in range(KT):
                            square(0, 0, k, 0)
                        for k in range(KT):
                            silu_gate(0, k)
                            silu_ln(0, 0, k)
                        for k in range(KT):
                            split_hi(0, k, 0)
                        for k in range(KT):
                            square(1, 1, k, 1)
                    if before >= 1:
                        scale_out(n - 1, 1 - slot)
                    if after >= 1:
                        for k in range(KT):
                            silu_gate(n + 1, k)
                    squares(n, slot, 0, before)
                    if after >= 1:
                        for k in range(KT):
                            silu_ln(n + 1, 1 - slot, k)
                    squares(n, slot, 1, before)
                    squares(n, slot, 2, before)
                    for k in range(KT):
                        if after >= 2:
                            square(n + 2, slot, k, before + 2)
                        if after >= 1:
                            split_hi(n + 1, k, before + 1)
                    squares(n, slot, 3, before)

                chunks(act, body, NCH, HEAD, TAIL)
                scale_out(NCH - 1, (NCH - 1) % 2)

            @block.vector
            def _(dve):
                def centre(n, slot, k):
                    if k == 0:
                        dve.wait_ge(mean_ready, n + 1)
                    dve.tensor_tensor(z[:, slot, k, :], z[:, slot, k, :], mean_ps[:], ALU.subtract).then_inc(centred, 1)

                def add_square(n, k, before):
                    if k == 0:
                        return
                    dve.wait_ge(sq_ready, n * KT + k + 1)
                    if k == 1:
                        if before >= 1:
                            dve.wait_ge(var_ready, n)
                        ins = dve.tensor_tensor(sq_sum[:], sq[:, 0, :], sq[:, 1, :], ALU.add)
                    else:
                        dve.wait_ge(sq_step, n * SUMS + k - 1)
                        ins = dve.tensor_tensor(sq_sum[:], sq_sum[:], sq[:, k % 2, :], ALU.add)
                    ins.then_inc(sq_step, 1)

                def normalise(n, slot, before):
                    dve.wait_ge(var_ready, n + 1)
                    if before >= 1:
                        dve.wait_ge(z_ready, n * KT)
                    dve.tensor_scalar(ln_var[:], var_ps[:], EPS, None, ALU.add).then_inc(rs_step, 1)
                    step = n * (RSQRT_STEPS + 1) + 1
                    dve.wait_ge(rs_step, step)
                    rsqrt(dve, rs_step, step, ln_rstd[:], ln_var[:], ln_tmp[:])

                def scale(n, slot, k):
                    dve.wait_ge(sq_ready, n * KT + k + 1)
                    dve.tensor_tensor(z[:, slot, k, :], z[:, slot, k, :], ln_rstd[:], ALU.mult).then_inc(z_ready, 1)

                def gate_y(n, slot, k):
                    dve.wait_ge(sg_ready, n * KT + k + 1)
                    dve.wait_ge(ln_ready, n * KT + k + 1)
                    dve.tensor_tensor(y[:, k, :], y[:, k, :], z[:, slot, k, :], ALU.mult).then_inc(y_ready, 1)

                def split_y(n, k):
                    dve.wait_ge(hi_ready, n * KT + k + 1)
                    dve.tensor_tensor(y_lo[:, k, :], y[:, k, :], f32v(y_hi[:, k, :]), ALU.subtract).then_inc(lo_ready, 1)

                def residual(n, slot, s):
                    if s == TPC - 1:
                        dve.wait_ge(y_used, (n + 1) * KT)
                    else:
                        dve.wait_ge(out_ready, n * (TPC - 1) + s + 1)
                    if s == 0:
                        dve.wait_ge(xr_loaded[slot], 8 * TPC * (n + 2 - slot))
                    dve.tensor_tensor(xr[:, slot, s, :], xr[:, slot, s, :], out_ps[:, s % 2].rearrange("p h c -> p (h c)"), ALU.add).then_inc(x2_ready, 1)

                def final_norm(n, before):
                    dve.wait_ge(ss_ready, (n + 1) * TPC)
                    if before >= 1:
                        dve.wait_ge(fin_scaled, n * TPC)
                    dve.tensor_scalar(fin_var[:], ss[:], 1.0 / D, EPS, ALU.mult, ALU.add).then_inc(fin_step, 1)
                    step = n * (RSQRT_STEPS + 1) + 1
                    dve.wait_ge(fin_step, step)
                    rsqrt(dve, fin_step, step, fin_rstd[:], fin_var[:], fin_tmp[:])

                def body(n, slot, before, after):
                    if before == 0:
                        for m in range(2):
                            for k in range(KT):
                                centre(m, m, k)
                                if k >= 1:
                                    add_square(m, k - 1, m)
                            add_square(m, KT - 1, m)
                            if m == 0:
                                normalise(0, 0, 0)
                                for k in range(KT):
                                    scale(0, 0, k)
                                for k in range(KT):
                                    gate_y(0, 0, k)
                                for k in range(KT):
                                    split_y(0, k)
                    if before >= 1:
                        final_norm(n - 1, before - 1)
                    if after >= 1:
                        normalise(n + 1, 1 - slot, before + 1)
                    residual(n, slot, 0)
                    if after >= 1:
                        for k in range(KT):
                            scale(n + 1, 1 - slot, k)
                    residual(n, slot, 1)
                    if after >= 1:
                        for k in range(KT):
                            gate_y(n + 1, 1 - slot, k)
                    residual(n, slot, 2)
                    for k in range(KT):
                        if after >= 2:
                            centre(n + 2, slot, k)
                        if after >= 2 and k >= 1:
                            add_square(n + 2, k - 1, before + 2)
                        if after >= 1:
                            split_y(n + 1, k)
                    if after >= 2:
                        add_square(n + 2, KT - 1, before + 2)
                    residual(n, slot, 3)

                chunks(dve, body, NCH, HEAD, TAIL)
                final_norm(NCH - 1, 9)


def kernel(**inputs):
    import concourse.bacc as bacc
    from concourse.bass_utils import run_bass_kernel_spmd

    nc = bacc.Bacc("TRN2", target_bir_lowering=False, num_devices=1)
    names = ["x", "c", "ctx", "c_ctx", "ap_ada_w", "ap_ada_b", "ap_norm_g", "ap_w_in", "ap_w_out", "ap_sink",
             "ap_pool_w", "ap_pool_scale", "cv_ada_w", "cv_ada_b", "cv_norm_g", "cv_w_in", "cv_w_out", "cv_dw_w",
             "cv_dw_b", "cv_ln_g", "cv_ln_b", "final_norm_g"]
    arrays = {"in_" + n: np.ascontiguousarray(inputs[n]) for n in names}
    arrays["rope"] = rope_tables()
    arrays["counts"] = pool_counts()
    arrays["masks"] = band_masks()
    aps = [nc.dram_tensor(n, a.shape, mybir.dt.from_np(a.dtype), kind="ExternalInput").ap() for n, a in arrays.items()]
    out = nc.dram_tensor("out", (1, SEQ, D), F32, kind="ExternalOutput").ap()
    build(nc, *aps, out)
    r = run_bass_kernel_spmd(nc, [arrays], core_ids=[0])
    return r.results[0]["out"]
```

```python
import numpy as np
import concourse.bass as bass
from concourse import mybir
from contextlib import ExitStack

F32 = mybir.dt.float32
F32R = mybir.dt.float32r
BF16 = mybir.dt.bfloat16
I32 = mybir.dt.int32
ALU = mybir.AluOpType
ACT = mybir.ActivationFunctionType
AXIS = mybir.AxisListType

P = 128
D = 1024
KT = D // P
SEQ = 4096
CTX = 256
GRID_W = 64
HD = 64
NQ = 8
NKV = 2
GRP = NQ // NKV
ATTN = NQ * HD
KV = NKV * HD
POOL_WINDOWS = (2, 4, 8, 16)
POOL = D - ATTN
CONV_K = 31
HALO = CONV_K // 2
EPS = 1e-6
NEG = -1e30
SCALE = HD ** -0.5
QKV = ATTN + 2 * KV
WIN = 3 * P
KEYS = WIN + CTX
CW = 512
NCH = SEQ // CW
TPC = CW // P
TILES = SEQ // P
KPAD = CTX + P + SEQ + P
PHALO = max(POOL_WINDOWS) // 2
UPAD = SEQ + 2 * PHALO
CPAD = SEQ + 2 * HALO
PAIR = 2 * CW
RSQRT_MAGIC = 0x5F3759DF
RSQRT_STEPS = 14


def rope_tables():
    rows = SEQ // GRID_W
    pairs = HD // 4
    row = np.repeat(np.arange(rows, dtype=np.float32), GRID_W)
    col = np.tile(np.arange(GRID_W, dtype=np.float32), rows)
    inv = np.float32(10000.0) ** (-np.arange(pairs, dtype=np.float32) / np.float32(pairs))
    ang = np.concatenate([row[:, None] * inv, col[:, None] * inv], axis=-1).astype(np.float32)
    cs = np.concatenate([np.ones((CTX, HD // 2), np.float32), np.cos(ang)])
    sn = np.concatenate([np.zeros((CTX, HD // 2), np.float32), np.sin(ang)])
    return np.stack([cs, sn], axis=1).astype(np.float32)


def pool_counts():
    t = np.arange(SEQ)
    out = [1.0 / (np.clip(t + w // 2, 0, SEQ) - np.clip(t - w // 2, 0, SEQ)) for w in POOL_WINDOWS]
    return np.stack(out).astype(np.float32)


def band_masks():
    r = np.arange(P)[:, None]
    c = np.arange(WIN)[None, :]
    inner = np.where(np.abs(c - P - r) <= P, 0.0, NEG)
    first = np.where(c < P, NEG, inner)
    last = np.where(c >= 2 * P, NEG, inner)
    return np.stack([first, inner, last], axis=1).astype(np.float32)


def build(nc, x, c, ctx_in, c_ctx, ap_ada_w, ap_ada_b, ap_norm_g, ap_w_in, ap_w_out, ap_sink,
          ap_pool_w, ap_pool_scale, cv_ada_w, cv_ada_b, cv_norm_g, cv_w_in, cv_w_out, cv_dw_w,
          cv_dw_b, cv_ln_g, cv_ln_b, final_norm_g, rope, counts, masks, out):
    scratch = lambda name, shape: nc.dram_tensor(name, shape, F32).ap()
    qT_d = scratch("qT_d", [NQ, P, CTX + SEQ])
    kT_d = scratch("kT_d", [2 * NKV, P, KPAD])
    v_d = scratch("v_d", [KPAD, 2, KV])
    aT_d = scratch("aT_d", [ATTN, SEQ])
    uT_d = scratch("uT_d", [POOL, UPAD])
    gT_d = scratch("gT_d", [D, SEQ])
    x1_d = scratch("x1_d", [SEQ, D])
    gate_d = scratch("gate_d", [2, D])
    cuT_d = scratch("cuT_d", [D, CPAD])
    ccT_d = scratch("ccT_d", [D, SEQ])
    cgT_d = scratch("cgT_d", [D, SEQ])

    whole = ExitStack()
    with whole:
        def persistent(name, shape, dt=F32):
            return whole.enter_context(nc.sbuf_tensor(name, shape, dt))

        ident = persistent("ident", [P, P])
        ident16 = persistent("ident16", [P, P], BF16)
        G = persistent("G", [P, 3, KT])
        S = persistent("S", [P, 3, KT])
        rstd0 = persistent("rstd0", [P, (CTX + SEQ) // P])
        rstd1 = persistent("rstd1", [P, TILES])
        conv_w = persistent("conv_w", [P, KT, CONV_K])
        conv_b = persistent("conv_b", [P, KT])
        conv_w_loaded = whole.enter_context(nc.semaphore("conv_w_loaded"))

        used = []

        def new_sem(stack, name):
            handle = stack.enter_context(nc.semaphore(name))
            used.append(handle)
            return handle

        def clear_semaphores():
            with nc.Block() as block:
                @block.gpsimd
                def _(pool):
                    for handle in used:
                        pool.sem_clear(handle)
            used.clear()

        def rsqrt(dve, step, n0, dst, v, tmp):
            n = n0

            def then(ins):
                nonlocal n
                ins.then_inc(step, 1)
                n = n + 1
                dve.wait_ge(step, n)

            then(dve.tensor_scalar(tmp.bitcast(I32), v.bitcast(I32), 1, None, ALU.logical_shift_right))
            then(dve.tensor_scalar(dst.bitcast(I32), tmp.bitcast(I32), -1.0, float(RSQRT_MAGIC), ALU.mult, ALU.add))
            for _ in range(3):
                then(dve.tensor_tensor(tmp, dst, dst, ALU.mult))
                then(dve.tensor_tensor(tmp, tmp, v, ALU.mult))
                then(dve.tensor_scalar(tmp, tmp, -0.5, 1.5, ALU.mult, ALU.add))
                then(dve.tensor_tensor(dst, dst, tmp, ALU.mult))

        def product(pe, acc, left, right, first, last):
            (lh, ll), (rh, rl) = left, right
            pe.matmul(acc, lh, rh, start=first, stop=False)
            pe.matmul(acc, lh, rl, start=False, stop=False)
            return pe.matmul(acc, ll, rh, start=False, stop=last)

        def f32v(ap):
            return ap.bitcast(F32)

        class BackgroundWeights:

            def __init__(self, name, keep, stage, source, width, piece):
                self.hi = keep.enter_context(nc.sbuf_tensor(name + "w_hi", [P, KT, width], F32R))
                self.lo = keep.enter_context(nc.sbuf_tensor(name + "w_lo", [P, KT, width], F32R))
                self.raw = stage.enter_context(nc.sbuf_tensor(name + "w_raw", [P, 2, piece], F32))
                self.loaded = [whole.enter_context(nc.semaphore(f"{name}w_loaded{i}")) for i in range(2)]
                self.hi_ready = new_sem(stage, name + "w_hi_ready")
                self.split = new_sem(stage, name + "w_split")
                self.pieces = [(source(k)[:, at:at + piece], k, slice(at, at + piece))
                               for k in range(KT) for at in range(0, width, piece)]

            def run(self, pool):
                def load(p):
                    pool.dma_start(self.raw[:, p % 2, :], self.pieces[p][0]).then_inc(self.loaded[p % 2], 16)

                load(0)
                load(1)
                for p, (_, k, cols) in enumerate(self.pieces):
                    pool.wait_ge(self.loaded[p % 2], 16 * (p // 2 + 1))
                    pool.tensor_copy(self.hi[:, k, cols], self.raw[:, p % 2, :]).then_inc(self.hi_ready, 1)
                    pool.wait_ge(self.hi_ready, p + 1)
                    pool.tensor_tensor(self.lo[:, k, cols], self.raw[:, p % 2, :], f32v(self.hi[:, k, cols]),
                                       ALU.subtract).then_inc(self.split, 1)
                    if p + 2 < len(self.pieces):
                        pool.wait_ge(self.split, p + 1)
                        load(p + 2)
                pool.wait_ge(self.split, len(self.pieces))

        qkv_keep = whole.enter_context(ExitStack())
        with ExitStack() as stage:
            qkv_w = BackgroundWeights("qkv_", qkv_keep, stage, lambda k: ap_w_in[0, k * P:(k + 1) * P, 0:QKV], QKV, QKV)
            sb = lambda n, s, d=F32: stage.enter_context(nc.sbuf_tensor(n, s, d))
            ps = lambda n, s, d=F32: stage.enter_context(nc.psum_tensor(n, s, d))
            sem = lambda n: new_sem(stage, n)
            zeros = sb("zeros", [P, 2 * KV])
            cond = sb("cond", [P, KT, 2])
            scond = sb("scond", [P, KT, 2])
            adab = sb("adab", [P, 2, 2 * KT])
            normg = sb("normg", [P, 2, KT])
            gbias = sb("gbias", [1, 2, D])
            gate = sb("gate", [1, 2, D])
            NAS = 4
            adaw = sb("adaw", [P, NAS, 3 * D])
            partial = sb("partial", [P, 3, 2 * D])
            ones = sb("ones", [P, 1])
            cols_ps = ps("cols_ps", [P, 3, 2 * KT])
            gate_ps = ps("gate_ps", [1, 2, 512])
            small_loaded = sem("small_loaded")
            zeroed = sem("zeroed")
            padded = sem("padded")
            ident_made = sem("ident_made")
            cond_ready = sem("cond_ready")
            adaw_loaded = [sem(f"adaw_loaded{i}") for i in range(NAS)]
            gate_added = sem("gate_added")
            small_issued = sem("small_issued")
            cols_ready = sem("cols_ready")
            gate_stored = sem("gate_stored")
            partial_step = sem("partial_step")
            vec_step = sem("vec_step")
            block = stage.enter_context(nc.Block())

            def after(n):
                return n + min(n, KT)

            @block.sync
            def _(sp):
                sp.wait_ge(small_issued, 1)
                for r, src in enumerate((ap_ada_w, cv_ada_w)):
                    for k in range(KT):
                        n = r * KT + k
                        if n >= NAS:
                            sp.wait_ge(gate_added, n - NAS + 1)
                            sp.wait_ge(partial_step, after(n - NAS + 1))
                        sp.dma_start(adaw[:, n % NAS, :], src[0, k * P:(k + 1) * P, :]).then_inc(adaw_loaded[n % NAS], 16)
                sp.wait_ge(vec_step, 4)
                sp.dma_start(gate_d.rearrange("(a r) d -> a r d", a=1), gate[:]).then_inc(gate_stored, 16)
                sp.wait_ge(gate_stored, 16)

            @block.gpsimd
            def _(pool):
                pool.memset(ident[:], 0.0).then_inc(ident_made, 1)
                pool.memset(ident16[:], 0.0).then_inc(ident_made, 1)
                pool.wait_ge(ident_made, 2)
                for m in (ident, ident16):
                    pool.affine_select(out=m[:], in_=m[:], compare_op=ALU.not_equal, fill=1.0, base=0,
                                       pattern=[[-1, P]], channel_multiplier=1).then_inc(ident_made, 1)
                pool.memset(ones[:], 1.0)
                pool.memset(zeros[:], 0.0).then_inc(zeroed, 1)
                pool.wait_ge(zeroed, 1)
                qkv_w.run(pool)

            @block.scalar
            def _(act):
                by_channel = lambda v: v.rearrange("(k p) -> p k", p=P)
                smalls = [(cond[:, :, 0], by_channel(c[0, :])), (cond[:, :, 1], by_channel(c_ctx)),
                          (adab[:, 0, :], by_channel(ap_ada_b[0, 0:2 * D])), (adab[:, 1, :], by_channel(cv_ada_b[0, 0:2 * D])),
                          (normg[:, 0, :], by_channel(ap_norm_g[0, :])), (normg[:, 1, :], by_channel(cv_norm_g[0, :])),
                          (gbias[:, 0, :], ap_ada_b[0:1, 2 * D:3 * D]),
                          (gbias[:, 1, :], cv_ada_b[0:1, 2 * D:3 * D])]
                for dst, src in smalls:
                    act.dma_start(dst, src, allow_slow_non_contiguous=True).then_inc(small_loaded, 16)
                act.sem_inc(small_issued, 1)
                act.wait_ge(small_loaded, 16 * len(smalls))
                act.activation(scond[:], cond[:], ACT.Silu).then_inc(cond_ready, 1)
                act.wait_ge(zeroed, 1)
                pads = []
                for at in (CTX, CTX + P + SEQ):
                    pads += [(kT_d[n, :, at:at + P], zeros[:, 0:P]) for n in range(2 * NKV)]
                    pads += [(v_d[at:at + P, :, :], zeros[:].rearrange("p (a d) -> p a d", a=2))]
                for t in range(POOL // P):
                    for at in (0, PHALO + SEQ):
                        pads.append((uT_d[t * P:(t + 1) * P, at:at + PHALO], zeros[:, 0:PHALO]))
                for t in range(KT):
                    for at in (0, HALO + SEQ):
                        pads.append((cuT_d[t * P:(t + 1) * P, at:at + HALO], zeros[:, 0:HALO]))
                for dst, src in pads:
                    act.dma_start(dst, src).then_inc(padded, 16)
                act.wait_ge(padded, 16 * len(pads))

            @block.tensor
            def _(pe):
                pe.wait_ge(cond_ready, 1)
                pe.wait_ge(zeroed, 1)
                for r in range(2):
                    for k in range(KT):
                        n = r * KT + k
                        slot = n % NAS
                        pe.wait_ge(adaw_loaded[slot], 16 * (n // NAS + 1))
                        if n == KT:
                            pe.wait_ge(vec_step, 2)
                        for h in range(2):
                            last = pe.matmul(gate_ps[:, h, :], scond[:, k, 0:1], adaw[:, slot, 2 * D + 512 * h:2 * D + 512 * (h + 1)],
                                             start=(k == 0), stop=(k == KT - 1))
                        last.then_inc(gate_added, 1)
                for m, tiles in ((0, KT), (1, KT), (2, 2 * KT)):
                    pe.wait_ge(partial_step, after(tiles))
                    for t in range(2 * KT):
                        last = pe.matmul(cols_ps[:, m, t:t + 1], partial[:, m, t * P:(t + 1) * P], ones[:], start=True, stop=True)
                    last.then_inc(cols_ready, 1)

            @block.vector
            def _(dve):
                dve.wait_ge(small_loaded, 16 * 8)
                dve.wait_ge(cond_ready, 1)
                for r in range(2):
                    for k in range(KT):
                        n = r * KT + k
                        slot = n % NAS
                        dve.wait_ge(adaw_loaded[slot], 16 * (n // NAS + 1))
                        if k >= 1:
                            dve.wait_ge(partial_step, after(n))
                        for m, v in (((0, 0), (1, 1)), ((2, 0),))[r]:
                            if k == 0:
                                ins = dve.tensor_scalar(partial[:, m, :], adaw[:, slot, 0:2 * D], scond[:, k, v:v + 1], None, ALU.mult)
                            else:
                                ins = dve.scalar_tensor_tensor(partial[:, m, :], adaw[:, slot, 0:2 * D], scond[:, k, v:v + 1],
                                                               partial[:, m, :], ALU.mult, ALU.add)
                            ins.then_inc(partial_step, 1)
                    dve.wait_ge(gate_added, (r + 1) * KT)
                    for h in range(2):
                        dve.tensor_tensor(gate[:, r, 512 * h:512 * (h + 1)], gate_ps[:, h, :],
                                          gbias[:, r, 512 * h:512 * (h + 1)], ALU.add).then_inc(vec_step, 1)
                step = 4
                for m, r in enumerate((0, 0, 1)):
                    dve.wait_ge(cols_ready, 3)
                    dve.tensor_tensor(S[:, m, :], cols_ps[:, m, 0:KT], adab[:, r, 0:KT], ALU.add)
                    dve.tensor_tensor(G[:, m, :], cols_ps[:, m, KT:2 * KT], adab[:, r, KT:2 * KT], ALU.add).then_inc(vec_step, 1)
                    step += 1
                    dve.wait_ge(vec_step, step)
                    dve.scalar_tensor_tensor(G[:, m, :], G[:, m, :], 1.0, normg[:, r, :], ALU.add, ALU.mult).then_inc(vec_step, 1)
                    step += 1
                dve.wait_ge(vec_step, step)

        def split_weights(name, pieces, hi, lo, scale_by=None, early=None):
            width = sum(w for _, _, w in pieces)
            with ExitStack() as stage:
                raw = stage.enter_context(nc.sbuf_tensor(name + "_raw", [P, 3, width], F32))
                loaded = [new_sem(stage, f"{name}_loaded{i}") for i in range(3)]
                raw_free = new_sem(stage, name + "_raw_free")
                hi_ready = new_sem(stage, name + "_hi_ready")
                scaled = new_sem(stage, name + "_scaled")
                if scale_by is not None:
                    row, row_loaded, row_src = scale_by
                block = stage.enter_context(nc.Block())
                n_k = hi.shape[1]

                @block.sync
                def _(sp):
                    sp.sem_inc(raw_free, 3)
                    if scale_by is not None:
                        sp.dma_start(row[:], row_src).then_inc(row_loaded, 16)
                    for k in range(n_k):
                        sp.wait_ge(raw_free, k + 1)
                        for at, src, w in pieces:
                            sp.dma_start(raw[:, k % 3, at:at + w], src(k)).then_inc(loaded[k % 3], 16)
                    if early is not None:
                        early(sp)

                @block.scalar
                def _(act):
                    for k in range(n_k):
                        act.wait_ge(loaded[k % 3], 16 * len(pieces) * (k // 3 + 1))
                        if scale_by is not None:
                            act.wait_ge(scaled, k + 1)
                        act.activation(hi[:, k, :], raw[:, k % 3, :], ACT.Copy).then_inc(hi_ready, 1)

                @block.vector
                def _(dve):
                    def fold(k):
                        dve.wait_ge(loaded[k % 3], 16 * len(pieces) * (k // 3 + 1))
                        dve.tensor_tensor(raw[:, k % 3, :], raw[:, k % 3, :], row[:], ALU.mult).then_inc(scaled, 1)

                    if scale_by is not None:
                        dve.wait_ge(row_loaded, 16)
                        fold(0)
                    for k in range(n_k):
                        if scale_by is not None and k + 1 < n_k:
                            fold(k + 1)
                        dve.wait_ge(hi_ready, k + 1)
                        dve.tensor_tensor(lo[:, k, :], raw[:, k % 3, :], f32v(hi[:, k, :]), ALU.subtract).then_inc(raw_free, 1)

        def chunks(eng, body, count, head, tail):
            for n in range(head):
                body(n, n % 2, n, count - 1 - n)
            with eng.Fori(0, (count - head - tail) // 2) as i:
                for n in (head, head + 1):
                    body(i * 2 + n, n % 2, n, tail)
            for n in range(count - tail, count):
                body(n, n % 2, n, count - 1 - n)

        turns = whole.enter_context(nc.semaphore("turns"))

        def at_turn(sp, sem, value):
            sp.wait_ge(sem, value)
            sp.sem_inc(turns, 1)

        clear_semaphores()
        with ExitStack() as stage:
            sb = lambda n, s, d=F32: stage.enter_context(nc.sbuf_tensor(n, s, d))
            ps = lambda n, s, d=F32: stage.enter_context(nc.psum_tensor(n, s, d))
            sem = lambda n: new_sem(stage, n)
            w_hi, w_lo = qkv_w.hi, qkv_w.lo
            T2 = 256
            SUB = T2 // P
            NH = NQ + NKV
            xin = sb("s1_x", [P, 2, SUB, D])
            junk = sb("s1_junk", [P, D])
            ss = sb("s1_ss", [P, 2, SUB])
            var = sb("s1_var", [P, SUB])
            tmp = sb("s1_tmp", [P, SUB])
            cs = sb("s1_rope", [P, 2, SUB, 2, HD // 2])
            xT = sb("s1_xT", [P, KT, T2])
            xT_hi = sb("s1_xT_hi", [P, 2, KT, T2], F32R)
            xT_lo = sb("s1_xT_lo", [P, 2, KT, T2], F32R)
            rot_c = sb("s1_rot_c", [P, NH, 2, HD // 2])
            rot_s = sb("s1_rot_s", [P, NH, 2, HD // 2])
            rot = sb("s1_rot", [P, NH, 2, HD // 2])
            q_sp = sb("s1_q_sp", [P, 2, NQ, 2, HD], F32R)
            k_sp = sb("s1_k_sp", [P, 2, 2, NKV, 2, HD], F32R)
            v_sp = sb("s1_v_sp", [P, 2, 2, KV], F32R)
            NT = NQ + 2 * NKV
            qk_t = sb("s1_qk_t", [P, 2, NT, P])
            tr_ps = ps("s1_tr_ps", [P, 2, 2, T2])
            qkv_ps = ps("s1_qkv_ps", [P, 2, 2, 512])
            out_ps = ps("s1_out_ps", [P, 2, 4, P])
            x_loaded = [sem(f"s1_x_loaded{i}") for i in range(2)]
            rope_loaded = [sem(f"s1_rope_loaded{i}") for i in range(2)]
            ss_ready = sem("s1_ss_ready")
            rs_step = sem("s1_rs_step")
            xn_ready = sem("s1_xn_ready")
            tr_ready = sem("s1_tr_ready")
            xT_ready = sem("s1_xT_ready")
            hi_ready = sem("s1_hi_ready")
            split_ready = sem("s1_split_ready")
            qkv_ready = sem("s1_qkv_ready")
            rot_step = sem("s1_rot_step")
            v_ready = sem("s1_v_ready")
            heads_split = sem("s1_heads_split")
            v_stored = [sem(f"s1_v_stored{i}") for i in range(2)]
            heads_ready = sem("s1_heads_ready")
            heads_out = sem("s1_heads_out")
            heads_stored = [sem(f"s1_heads_stored{i}") for i in range(2)]
            block = stage.enter_context(nc.Block())
            CHUNKS = 1 + SEQ // T2
            HEAD, TAIL = 3, 2
            BANKS = KT // 2
            OUTS = NT // 4

            @block.sync
            def _(sp):
                def load(n, slot, before):
                    if before >= 2:
                        at_turn(sp, tr_ready, (n - 1) * BANKS)
                    src = ctx_in[0, :, :] if before == 0 else x[0, bass.ds((n - 1) * T2, T2), :]
                    sp.dma_start(xin[:, slot], src.rearrange("(s p) d -> p s d", p=P)).then_inc(x_loaded[slot], 16)

                def load_rope(n, slot, before):
                    if before >= 2:
                        at_turn(sp, heads_split, (n - 1) * SUB)
                    sp.dma_start(cs[:, slot], rope[bass.ds(n * T2, T2), :, :].rearrange("(s p) a d -> p s a d", p=P)).then_inc(rope_loaded[slot], 16)

                def store(n, s, is_ctx):
                    u = n * SUB + s
                    col = n * T2 + s * P
                    key = col + (0 if is_ctx else P)
                    at_turn(sp, v_ready, u + 1)
                    sp.dma_start(v_d[bass.ds(key, P), :, :], f32v(v_sp[:, s])).then_inc(v_stored[s], 16)
                    at_turn(sp, heads_out, (u + 1) * OUTS)
                    sp.dma_start(qT_d[:, :, bass.ds(col, P)].rearrange("h p t -> p h t"), qk_t[:, s, 0:NQ, :]).then_inc(heads_stored[s], 16)
                    sp.dma_start(kT_d[:, :, bass.ds(key, P)].rearrange("h p t -> p h t"), qk_t[:, s, NQ:NT, :]).then_inc(heads_stored[s], 16)

                def body(n, slot, before, after):
                    if before == 0:
                        load(0, 0, 0)
                        load(1, 1, 1)
                        load_rope(0, 0, 0)
                    if after >= 2:
                        load(n + 2, slot, before + 2)
                    if after >= 1:
                        load_rope(n + 1, 1 - slot, before + 1)
                    if before >= 1:
                        store(n - 1, 1, before == 1)
                    store(n, 0, before == 0)

                chunks(sp, body, CHUNKS, HEAD, TAIL)
                store(CHUNKS - 1, 1, False)
                for s in range(SUB):
                    sp.wait_ge(v_stored[s], 16 * CHUNKS)
                    sp.wait_ge(heads_stored[s], 32 * CHUNKS)

            @block.scalar
            def _(act):
                def squares(n, slot, before):
                    act.wait_ge(x_loaded[slot], 8 * (n + 2 - slot))
                    for s in range(SUB):
                        if before + s > 0:
                            act.wait_ge(ss_ready, n * SUB + s)
                        act.activation(junk[:], xin[:, slot, s, :], ACT.Square,
                                       accum_out=ss[:, slot, s:s + 1]).then_inc(ss_ready, 1)

                def evacuate_xT(n, before):
                    which = 1 if before == 0 else 0
                    for b in range(BANKS):
                        act.wait_ge(tr_ready, n * BANKS + b + 1)
                        if b == 0 and before >= 1:
                            act.wait_ge(split_ready, 2 * n)
                        for kk in range(2):
                            k = 2 * b + kk
                            ins = act.activation(xT[:, k, :], tr_ps[:, b % 2, kk, :], ACT.Identity,
                                                 scale=G[:, which, k:k + 1], bias=S[:, which, k:k + 1])
                        ins.then_inc(xT_ready, 1)

                def evacuate_heads(n, s, before):
                    u = n * SUB + s
                    if before >= 1:
                        act.wait_ge(heads_stored[s], 32 * n)
                    for b in range(OUTS):
                        act.wait_ge(heads_ready, u * OUTS + b + 1)
                        act.activation(qk_t[:, s, 4 * b:4 * b + 4, :], out_ps[:, (s * OUTS + b) % 2], ACT.Copy).then_inc(heads_out, 1)

                def body(n, slot, before, after):
                    if before == 0:
                        squares(0, 0, 0)
                        squares(1, 1, 1)
                        evacuate_xT(0, 0)
                    if before >= 1:
                        evacuate_heads(n - 1, 1, before - 1)
                    if after >= 1:
                        evacuate_xT(n + 1, before + 1)
                    if after >= 2:
                        squares(n + 2, slot, before + 2)
                    evacuate_heads(n, 0, before)

                chunks(act, body, CHUNKS, HEAD, TAIL)
                evacuate_heads(CHUNKS - 1, 1, 9)

            @block.vector
            def _(dve):
                def normalise(n, slot, before):
                    if before >= 1:
                        dve.wait_ge(xn_ready, n)
                    dve.wait_ge(ss_ready, (n + 1) * SUB)
                    dve.tensor_scalar(var[:], ss[:, slot, :], 1.0 / D, EPS, ALU.mult, ALU.add).then_inc(rs_step, 1)
                    step = n * (RSQRT_STEPS + 1) + 1
                    dve.wait_ge(rs_step, step)
                    rs = rstd0[:, bass.ds(n * SUB, SUB)]
                    rsqrt(dve, rs_step, step, rs, var[:], tmp[:])
                    for s in range(SUB):
                        ins = dve.tensor_scalar(xin[:, slot, s, :], xin[:, slot, s, :], rstd0[:, bass.ds(n * SUB + s, 1)], None, ALU.mult)
                    ins.then_inc(xn_ready, 1)

                def split(n, slot, before):
                    if before >= 2:
                        dve.wait_ge(qkv_ready, (n - 1) * SUB)
                    for h in range(2):
                        ks = slice(4 * h, 4 * h + 4)
                        dve.wait_ge(xT_ready, n * BANKS + 2 * h + 2)
                        dve.tensor_copy(xT_hi[:, slot, ks], xT[:, ks]).then_inc(hi_ready, 1)
                        dve.wait_ge(hi_ready, n * 2 + h + 1)
                        dve.tensor_tensor(xT_lo[:, slot, ks], xT[:, ks], f32v(xT_hi[:, slot, ks]), ALU.subtract).then_inc(split_ready, 1)

                def rotate(n, slot, s, before):
                    u = n * SUB + s
                    q_in = qkv_ps[:, s, 0, :].rearrange("p (h a d) -> p h a d", a=2, d=HD // 2)
                    k_in = qkv_ps[:, s, 1, 0:KV].rearrange("p (h a d) -> p h a d", a=2, d=HD // 2)
                    v_in = qkv_ps[:, s, 1, KV:2 * KV]
                    dve.wait_ge(qkv_ready, u + 1)
                    dve.wait_ge(rope_loaded[slot], 8 * (n + 2 - slot))
                    if before >= 1:
                        dve.wait_ge(v_stored[s], 16 * n)
                    if before + s >= 1:
                        dve.wait_ge(heads_split, u)
                    for a, dst in ((0, rot_c), (1, rot_s)):
                        table = cs[:, slot, s, a, :].unsqueeze(1).unsqueeze(1)
                        dve.tensor_tensor(dst[:, 0:NQ], q_in, table.to_broadcast([P, NQ, 2, HD // 2]), ALU.mult)
                        dve.tensor_tensor(dst[:, NQ:NH], k_in, table.to_broadcast([P, NKV, 2, HD // 2]), ALU.mult)
                    dve.tensor_copy(v_sp[:, s, 0, :], v_in).then_inc(rot_step, 1)
                    dve.wait_ge(rot_step, u * 3 + 1)
                    dve.tensor_tensor(v_sp[:, s, 1, :], v_in, f32v(v_sp[:, s, 0, :]), ALU.subtract).then_inc(v_ready, 1)
                    dve.tensor_tensor(rot[:, :, 0, :], rot_c[:, :, 0, :], rot_s[:, :, 1, :], ALU.subtract)
                    dve.tensor_tensor(rot[:, :, 1, :], rot_c[:, :, 1, :], rot_s[:, :, 0, :], ALU.add).then_inc(rot_step, 1)
                    dve.wait_ge(rot_step, u * 3 + 2)
                    if before >= 1:
                        dve.wait_ge(heads_ready, (u - 1) * OUTS)
                    qr = rot[:, 0:NQ].rearrange("p h a d -> p h (a d)")
                    kr = rot[:, NQ:NH].rearrange("p h a d -> p h (a d)").unsqueeze(2).to_broadcast([P, NKV, 2, HD])
                    dve.tensor_copy(q_sp[:, s, :, 0, :], qr)
                    dve.tensor_copy(k_sp[:, s, 0], kr).then_inc(rot_step, 1)
                    dve.wait_ge(rot_step, u * 3 + 3)
                    dve.tensor_tensor(q_sp[:, s, :, 1, :], qr, f32v(q_sp[:, s, :, 0, :]), ALU.subtract)
                    dve.tensor_tensor(k_sp[:, s, 1], kr, f32v(k_sp[:, s, 0]), ALU.subtract).then_inc(heads_split, 1)

                def body(n, slot, before, after):
                    if before == 0:
                        normalise(0, 0, 0)
                        split(0, 0, 0)
                    if after >= 1:
                        normalise(n + 1, 1 - slot, before + 1)
                    rotate(n, slot, 0, before)
                    if after >= 1:
                        split(n + 1, 1 - slot, before + 1)
                    rotate(n, slot, 1, before)

                chunks(dve, body, CHUNKS, HEAD, TAIL)

            @block.tensor
            def _(pe):
                def transpose_x(n, slot, before):
                    pe.wait_ge(xn_ready, n + 1)
                    for b in range(BANKS):
                        if not (before == 0 and b < 2):
                            pe.wait_ge(xT_ready, n * BANKS + b - 1)
                        for kk in range(2):
                            k = 2 * b + kk
                            for s in range(SUB):
                                ins = pe.transpose(tr_ps[:, b % 2, kk, s * P:(s + 1) * P], xin[:, slot, s, k * P:(k + 1) * P], ident[:])
                        ins.then_inc(tr_ready, 1)

                def products(n, slot, s, before):
                    u = n * SUB + s
                    if s == 0:
                        pe.wait_ge(split_ready, 2 * (n + 1))
                    if before >= 1:
                        pe.wait_ge(v_ready, u - 1)
                    ts = slice(s * P, (s + 1) * P)
                    for k in range(KT):
                        x_parts = (xT_hi[:, slot, k, ts], xT_lo[:, slot, k, ts])
                        product(pe, qkv_ps[:, s, 0, :], x_parts, (w_hi[:, k, 0:ATTN], w_lo[:, k, 0:ATTN]), k == 0, k == KT - 1)
                        ins = product(pe, qkv_ps[:, s, 1, 0:2 * KV], x_parts, (w_hi[:, k, ATTN:QKV], w_lo[:, k, ATTN:QKV]), k == 0, k == KT - 1)
                    ins.then_inc(qkv_ready, 1)

                def heads(n, s, before):
                    u = n * SUB + s
                    pe.wait_ge(heads_split, u + 1)
                    for b in range(OUTS):
                        if not (before == 0 and s * OUTS + b < 2):
                            pe.wait_ge(heads_out, u * OUTS + b - 1)
                        for j in range(4):
                            h = 4 * b + j
                            src = q_sp[:, s, h] if h < NQ else k_sp[:, s, (h - NQ) // NKV, (h - NQ) % NKV]
                            ins = pe.transpose(out_ps[:, (s * OUTS + b) % 2, j, :], f32v(src.rearrange("p a d -> p (a d)")), ident[:])
                        ins.then_inc(heads_ready, 1)

                def body(n, slot, before, after):
                    if before == 0:
                        transpose_x(0, 0, 0)
                    products(n, slot, 0, before)
                    if before >= 1:
                        heads(n - 1, 1, before - 1)
                    if after >= 1:
                        transpose_x(n + 1, 1 - slot, before + 1)
                    products(n, slot, 1, before)
                    heads(n, 0, before)

                chunks(pe, body, CHUNKS, HEAD, TAIL)
                heads(CHUNKS - 1, 1, 9)

        qkv_keep.close()
        clear_semaphores()
        ug_keep = ExitStack()
        with ExitStack() as stage:
            ug_w = BackgroundWeights("ug_", ug_keep, stage, lambda k: ap_w_in[0, k * P:(k + 1) * P, QKV:], POOL + D, 512)
            sb = lambda n, s, d=F32: stage.enter_context(nc.sbuf_tensor(n, s, d))
            ps = lambda n, s, d=F32: stage.enter_context(nc.psum_tensor(n, s, d))
            sem = lambda n: new_sem(stage, n)
            q_in = sb("s2_q_in", [P, 2, NQ, P], F32R)
            k_in = sb("s2_k_in", [P, 2, 2 * NKV, WIN], F32R)
            v_in = sb("s2_v_in", [P, 2, 3, 2, KV], F32R)
            k_ctx = sb("s2_k_ctx", [P, 2 * NKV, CTX], F32R)
            v_ctx = sb("s2_v_ctx", [P, CTX // P, 2, KV], F32R)
            mask_in = sb("s2_mask_in", [P, 3, WIN])
            mask = sb("s2_mask", [P, 3, WIN], BF16)
            sink = sb("s2_sink", [P, NQ])
            neg_sink = sb("s2_neg_sink", [P, NQ])
            row_max = sb("s2_row_max", [P, 4, GRP])
            neg_max = sb("s2_neg_max", [P, 4, GRP])
            p_sum = sb("s2_p_sum", [P, 4, GRP])
            p_sink = sb("s2_p_sink", [P, 4, GRP])
            den = sb("s2_den", [P, 4, GRP])
            rden = sb("s2_rden", [P, 4, GRP])
            probs = sb("s2_probs", [P, 4, GRP, KEYS])
            pT_hi = sb("s2_pT_hi", [P, KEYS // P, 512], F32R)
            pT_lo = sb("s2_pT_lo", [P, KEYS // P, 512], F32R)
            o_sb = sb("s2_o_sb", [HD, 2, 512])
            s_ps = ps("s2_s_ps", [P, 2, 1024])
            pT_ps = ps("s2_pT_ps", [P, 2, 512])
            o_ps = ps("s2_o_ps", [P, 2, 512])
            fixed_loaded = sem("s2_fixed_loaded")
            mask_ready = sem("s2_mask_ready")
            qk_loaded = [sem(f"s2_qk_loaded{i}") for i in range(2)]
            v_loaded = [sem(f"s2_v_loaded{i}") for i in range(2)]
            s_ready = sem("s2_s_ready")
            max_ready = sem("s2_max_ready")
            neg_ready = sem("s2_neg_ready")
            p_ready = sem("s2_p_ready")
            norm_step = sem("s2_norm_step")
            p_scaled = sem("s2_p_scaled")
            pT_ready = sem("s2_pT_ready")
            hi_ready = sem("s2_hi_ready")
            lo_ready = sem("s2_lo_ready")
            pv_ready = sem("s2_pv_ready")
            o_ready = sem("s2_o_ready")
            o_stored = [sem(f"s2_o_stored{i}") for i in range(2)]
            block = stage.enter_context(nc.Block())
            KTILES = KEYS // P
            HEAD, TAIL = 3, 1

            @block.sync
            def _(sp):
                def load_qk(b, slot, before):
                    if before >= 2:
                        at_turn(sp, s_ready, (b - 1) * NQ)
                    sp.dma_start(f32v(q_in[:, slot]), qT_d[:, :, bass.ds(b * P + CTX, P)].rearrange("h p t -> p h t")).then_inc(qk_loaded[slot], 16)
                    sp.dma_start(f32v(k_in[:, slot]), kT_d[:, :, bass.ds(b * P + CTX, WIN)].rearrange("h p t -> p h t")).then_inc(qk_loaded[slot], 16)

                def load_v(b, slot, before):
                    if before >= 2:
                        at_turn(sp, pv_ready, (b - 1) * 2 * KTILES)
                    sp.dma_start(f32v(v_in[:, slot]), v_d[bass.ds(b * P + CTX, WIN), :, :].rearrange("(j p) a d -> p j a d", p=P)).then_inc(v_loaded[slot], 16)

                def store(b, y, g):
                    at_turn(sp, o_ready, y + 1)
                    rows = slice(g * GRP * HD, (g + 1) * GRP * HD)
                    sp.dma_start(aT_d[rows, bass.ds(b * P, P)].rearrange("(i d) t -> d i t", d=HD),
                                 o_sb[:, g, :].rearrange("d (i t) -> d i t", i=GRP)).then_inc(o_stored[g], 16)

                fixed = [(f32v(k_ctx[:]), kT_d[:, :, 0:CTX].rearrange("h p t -> p h t")),
                         (f32v(v_ctx[:]), v_d[0:CTX, :, :].rearrange("(j p) a d -> p j a d", p=P)),
                         (mask_in[:], masks), (sink[:], ap_sink[0:1, :].partition_broadcast(P))]
                load_qk(0, 0, 0)
                for dst, src in fixed:
                    sp.dma_start(dst, src).then_inc(fixed_loaded, 16)

                def body(b, slot, before, after):
                    if after >= 1:
                        load_qk(b + 1, 1 - slot, before + 1)
                    if before >= 2:
                        store(b - 2, 2 * b - 3, 1)
                    load_v(b, slot, before)
                    if before >= 1:
                        store(b - 1, 2 * b - 2, 0)

                chunks(sp, body, TILES, HEAD, TAIL)
                store(TILES - 2, 2 * TILES - 3, 1)
                for g in range(2):
                    store(TILES - 1, 2 * TILES - 2 + g, g)
                for g in range(2):
                    sp.wait_ge(o_stored[g], 16 * TILES)

            @block.gpsimd
            def _(pool):
                ug_w.run(pool)
                for t in range(KT):
                    pool.dma_start(conv_w[:, t, :], cv_dw_w[0, :, t * P:(t + 1) * P].rearrange("k p -> p k"),
                                   allow_slow_non_contiguous=True).then_inc(conv_w_loaded, 16)
                pool.dma_start(conv_b[:], cv_dw_b[0, :].rearrange("(t p) -> p t", p=P), allow_slow_non_contiguous=True).then_inc(conv_w_loaded, 16)
                pool.wait_ge(conv_w_loaded, 16 * (KT + 1))

            @block.tensor
            def _(pe):
                def scores(y, slot, g, i, variant, yb):
                    h = GRP * g + i
                    if yb * GRP + i >= 2:
                        pe.wait_ge(p_ready, y * GRP + i - 1)
                    acc = s_ps[:, i % 2, :]
                    pe.matmul(acc[:, P:512], ident16[:], mask[:, variant, :], start=True, stop=False)
                    for part, stop in ((0, False), (1, True)):
                        pe.matmul(acc[:, P:512], q_in[:, slot, h, :], k_in[:, slot, NKV * part + g, :], start=False, stop=stop)
                    for part in range(2):
                        ins = pe.matmul(acc[:, 512:512 + CTX], q_in[:, slot, h, :], k_ctx[:, NKV * part + g, :], start=part == 0, stop=part == 1)
                    ins.then_inc(s_ready, 1)

                def transpose_tile(y, ring, g, j, yb):
                    if j == 0:
                        pe.wait_ge(p_scaled, (y + 1) * GRP)
                    if yb * KTILES + j >= 2:
                        pe.wait_ge(lo_ready, y * KTILES + j - 1)
                    for i in range(GRP):
                        ins = pe.transpose(pT_ps[:, (g + j) % 2, i * P:(i + 1) * P], probs[:, ring, i, j * P:(j + 1) * P], ident[:])
                    ins.then_inc(pT_ready, 1)

                def values(b, y, slot, g, j, yb):
                    pe.wait_ge(lo_ready, y * KTILES + j + 1)
                    if j == 0 and yb >= 2:
                        pe.wait_ge(o_ready, y - 1)
                    if j == 0 and g == 0:
                        pe.wait_ge(v_loaded[slot], 8 * (b + 2 - slot))
                    v = v_in[:, slot, j] if j < 3 else v_ctx[:, j - 3]
                    cols = slice(HD * g, HD * (g + 1))
                    product(pe, o_ps[0:HD, g, :], (v[:, 0, cols], v[:, 1, cols]),
                            (pT_hi[:, j, :], pT_lo[:, j, :]), j == 0, j == KTILES - 1).then_inc(pv_ready, 1)

                def turn(b, slot, g, before, variant, new=True, steps=KTILES):
                    y, yb = 2 * b + g, 2 * before + g
                    for i in range(steps):
                        if new and i < GRP:
                            scores(y, slot, g, i, variant, yb)
                        if steps == KTILES and yb >= 2:
                            transpose_tile(y - 2, (2 * slot + g + 2) % 4, g, i, yb - 2)
                        if i < 2 and yb >= 3:
                            b3, slot3 = (b - 2, slot) if g == 0 else (b - 1, 1 - slot)
                            values(b3, y - 3, slot3, 1 - g, KTILES - 2 + i, yb - 3)
                        elif i >= 2 and yb >= 2:
                            values(b - 1, y - 2, 1 - slot, g, i - 2, yb - 2)

                pe.wait_ge(mask_ready, 1)
                pe.wait_ge(fixed_loaded, 64)

                def body(b, slot, before, after):
                    variant = 0 if before == 0 else 2 if after == 0 else 1
                    pe.wait_ge(qk_loaded[slot], 16 * (b + 2 - slot))
                    for g in range(2):
                        turn(b, slot, g, before, variant)

                chunks(pe, body, TILES, HEAD, TAIL)
                turn(TILES, 0, 0, TILES, 0, new=False)
                turn(TILES, 0, 1, TILES, 0, new=False)
                turn(TILES + 1, 1, 0, TILES + 1, 0, new=False, steps=2)

            @block.scalar
            def _(act):
                act.wait_ge(fixed_loaded, 64)

                def exponentials(y, ring, g, i, yb):
                    e = y * GRP + i
                    h = GRP * g + i
                    act.wait_ge(neg_ready, e + 1)
                    if yb >= 4:
                        act.wait_ge(p_scaled, e - 4 * GRP + 1)
                        if i == 0:
                            act.wait_ge(pT_ready, (y - 3) * KTILES)
                    col = slice(i, i + 1)
                    act.activation(p_sink[:, ring, col], sink[:, h:h + 1], ACT.Exp, bias=neg_max[:, ring, col])
                    act.activation(probs[:, ring, i, :], s_ps[:, i % 2, P:P + KEYS], ACT.Exp, scale=SCALE,
                                   bias=neg_max[:, ring, col], accum_out=p_sum[:, ring, col]).then_inc(p_ready, 1)

                def split_hi(y, g, j, yb):
                    act.wait_ge(pT_ready, y * KTILES + j + 1)
                    if yb >= 1:
                        act.wait_ge(pv_ready, (y - 1) * KTILES + j + 1)
                    act.activation(pT_hi[:, j, :], pT_ps[:, (g + j) % 2, :], ACT.Copy).then_inc(hi_ready, 1)

                def evacuate(y, g, before):
                    act.wait_ge(pv_ready, (y + 1) * KTILES)
                    if before >= 1:
                        act.wait_ge(o_stored[g], 8 * (y - g))
                    act.activation(o_sb[:, g, :], o_ps[0:HD, g, :], ACT.Copy).then_inc(o_ready, 1)

                def turn(b, slot, g, before, new=True, steps=KTILES):
                    y, yb = 2 * b + g, 2 * before + g
                    for i in range(steps):
                        if new and i >= 1:
                            exponentials(y, 2 * slot + g, g, i - 1, yb)
                        if steps == KTILES and yb >= 2:
                            split_hi(y - 2, g, i, yb - 2)
                        if i == 2 and yb >= 3:
                            evacuate(y - 3, 1 - g, (yb - 3) // 2)

                def body(b, slot, before, after):
                    for g in range(2):
                        turn(b, slot, g, before)

                chunks(act, body, TILES, HEAD, TAIL)
                turn(TILES, 0, 0, TILES, new=False)
                turn(TILES, 0, 1, TILES, new=False)
                evacuate(2 * TILES - 1, 1, TILES - 1)

            @block.vector
            def _(dve):
                dve.wait_ge(fixed_loaded, 64)
                dve.tensor_copy(mask[:], mask_in[:])
                dve.tensor_scalar(neg_sink[:], sink[:], -1.0, None, ALU.mult).then_inc(mask_ready, 1)
                dve.wait_ge(mask_ready, 1)

                def maxima(y, ring, i):
                    e = y * GRP + i
                    col = slice(i, i + 1)
                    dve.wait_ge(s_ready, e + 1)
                    dve.tensor_reduce(row_max[:, ring, col], s_ps[:, i % 2, P:P + KEYS], AXIS.X, ALU.max).then_inc(max_ready, 1)

                def negate(y, ring, g, i, yb):
                    e = y * GRP + i
                    h = GRP * g + i
                    col = slice(i, i + 1)
                    dve.wait_ge(max_ready, e + 1)
                    if yb >= 4:
                        dve.wait_ge(p_ready, e - 4 * GRP + 1)
                    dve.scalar_tensor_tensor(neg_max[:, ring, col], row_max[:, ring, col], -SCALE, neg_sink[:, h:h + 1],
                                             ALU.mult, ALU.min).then_inc(neg_ready, 1)

                def denominators(y, ring):
                    dve.wait_ge(p_ready, (y + 1) * GRP)
                    dve.tensor_tensor(den[:, ring, :], p_sum[:, ring, :], p_sink[:, ring, :], ALU.add).then_inc(norm_step, 1)

                def reciprocals(y, ring):
                    dve.wait_ge(norm_step, 2 * y + 1)
                    dve.reciprocal(rden[:, ring, :], den[:, ring, :]).then_inc(norm_step, 1)

                def scale(y, ring, i):
                    dve.wait_ge(norm_step, 2 * y + 2)
                    dve.tensor_scalar(probs[:, ring, i, :], probs[:, ring, i, :], rden[:, ring, i:i + 1], None, ALU.mult).then_inc(p_scaled, 1)

                def split_lo(y, g, j):
                    dve.wait_ge(hi_ready, y * KTILES + j + 1)
                    dve.tensor_tensor(pT_lo[:, j, :], pT_ps[:, (g + j) % 2, :], f32v(pT_hi[:, j, :]), ALU.subtract).then_inc(lo_ready, 1)

                def turn(b, slot, g, before, new=True):
                    y, yb = 2 * b + g, 2 * before + g
                    ring = 2 * slot + g
                    for i in range(KTILES):
                        if i == 0:
                            if yb >= 3:
                                split_lo(y - 3, 1 - g, KTILES - 1)
                        elif yb >= 2:
                            split_lo(y - 2, g, i - 1)
                        past = (ring + 3) % 4
                        scaling = yb >= 1 and (new or g == 0)
                        if new and i < GRP:
                            maxima(y, ring, i)
                        if scaling and i == 0:
                            denominators(y - 1, past)
                        if scaling and 1 <= i < GRP:
                            scale(y - 1, past, i - 1)
                        if new and i < GRP:
                            negate(y, ring, g, i, yb)
                        if scaling and i == 0:
                            reciprocals(y - 1, past)
                        if scaling and i == GRP:
                            scale(y - 1, past, GRP - 1)

                def body(b, slot, before, after):
                    for g in range(2):
                        turn(b, slot, g, before)

                chunks(dve, body, TILES, HEAD, TAIL)
                turn(TILES, 0, 0, TILES, new=False)
                turn(TILES, 0, 1, TILES, new=False)
                split_lo(2 * TILES - 1, 1, KTILES - 1)

        NT3 = 12
        BANKS3 = 6

        STEPS = 2 * CONV_K

        def conv_order(half, before):
            if before < 3:
                if half == 0:
                    return None
                return (0, ((2, 3), (0, 1), (2, 3))[before], ((2, 3, 3)[before] * 2 - before) * CW)
            return (half, (0, 1), -3 * CW) if before % 2 else (half, (2, 3), -4 * CW)

        class ConvTaps:

            CREDIT = 2 * STEPS

            def __init__(self, name, stage, off):
                sb = lambda n, s: stage.enter_context(nc.sbuf_tensor(name + n, s, F32))
                sem = lambda n: new_sem(stage, name + n)
                self.off = off
                self.u = sb("cu", [P, 2, 2, PAIR + 2 * HALO])
                self.acc = sb("cacc", [P, 2, 2, PAIR])
                self.u_loaded = [sem(f"cu_loaded{i}") for i in range(2)]
                self.step = sem("conv_step")
                self.acc_free = sem("acc_free")
                self.stored = [sem(f"conv_stored{i}") for i in range(2)]

            def give_credits(self, q):
                q.sem_inc(self.step, self.CREDIT)
                q.sem_inc(self.acc_free, 2)

            def load(self, q, n, slot, item, u_stored):
                o, set_, (half, tiles, at) = n - self.off, (slot + self.off) % 2, item
                at_turn(q, self.step, (o + 1) * STEPS)
                if u_stored is not None:
                    for i in range(2):
                        at_turn(q, u_stored[i], 32 * n - (16 if tiles == (0, 1) else 32))
                for i, t in enumerate(tiles):
                    rows = slice((4 * half + t) * P, (4 * half + t + 1) * P)
                    q.dma_start(self.u[:, set_, i, :], cuT_d[rows, bass.ds(n * CW + at, PAIR + 2 * HALO)]).then_inc(self.u_loaded[set_], 16)

            def run(self, dve, n, slot, before, item, quarter):
                o, set_, (half, tiles, at) = n - self.off, (slot + self.off) % 2, item
                if quarter == 0:
                    dve.wait_ge(self.u_loaded[set_], 16 * (o + 2 - set_))
                    dve.wait_ge(self.acc_free, o + 1)
                bounds = (0, 7, 15, 23, CONV_K)
                for tap in range(bounds[quarter], bounds[quarter + 1]):
                    for i, t in enumerate(tiles):
                        ch = 4 * half + t
                        acc = self.acc[:, set_, i, :]
                        u = self.u[:, set_, i, tap:tap + PAIR]
                        w = conv_w[:, ch, tap:tap + 1]
                        if tap == 0:
                            dve.tensor_scalar(acc, u, w, conv_b[:, ch:ch + 1], ALU.mult, ALU.add).then_inc(self.step, 1)
                        else:
                            dve.wait_ge(self.step, self.CREDIT + o * STEPS + 2 * tap + i - 1)
                            dve.scalar_tensor_tensor(acc, u, w, acc, ALU.mult, ALU.add).then_inc(self.step, 1)

            def store(self, q, n, slot, item):
                o, set_, (half, tiles, at) = n - self.off, (slot + self.off) % 2, item
                at_turn(q, self.step, self.CREDIT + (o + 1) * STEPS)
                for i, t in enumerate(tiles):
                    rows = slice((4 * half + t) * P, (4 * half + t + 1) * P)
                    q.dma_start(ccT_d[rows, bass.ds(n * CW + at, PAIR)], self.acc[:, set_, i, :]).then_inc(self.stored[set_], 16)
                q.wait_ge(self.stored[set_], 16 * (o + 2 - set_))
                q.sem_inc(self.acc_free, 1)

            def finish(self, q, items):
                for set_ in range(2):
                    q.wait_ge(self.stored[set_], 32 * ((items + 1 - set_) // 2))

        def project(name, x_rows, rstd, which, weights, half):
            conv = half is not None
            with ExitStack() as stage:
                sb = lambda n, s, d=F32: stage.enter_context(nc.sbuf_tensor(name + n, s, d))
                ps = lambda n, s, d=F32: stage.enter_context(nc.psum_tensor(name + n, s, d))
                sem = lambda n: new_sem(stage, name + n)
                xin = sb("x", [P, TPC, D])
                x_loaded = [sem(f"x_loaded{s}") for s in range(TPC)]

                def load_first_x(sp):
                    for s in range(TPC):
                        sp.dma_start(xin[:, s, :], x_rows[s * P:(s + 1) * P, :]).then_inc(x_loaded[s], 16)

                if conv:
                    w_hi = sb("w_hi", [P, KT, NT3 * P], F32R)
                    w_lo = sb("w_lo", [P, KT, NT3 * P], F32R)
                    split_weights(name + "w", weights, w_hi, w_lo, early=load_first_x)
                else:
                    w_hi, w_lo = weights.hi, weights.lo
                xT = sb("xT", [P, KT, CW])
                xT_hi = sb("xT_hi", [P, KT, CW], F32R)
                xT_lo = sb("xT_lo", [P, KT, CW], F32R)
                sig = sb("sig", [P, 2, CW]) if conv else None
                u_sb = sb("u_sb", [P, 2, CW])
                g_sb = sb("g_sb", [P, 2, CW])
                tr_ps = ps("tr_ps", [P, 2, CW])
                out_ps = ps("out_ps", [P, BANKS3, CW])
                xn_ready = sem("xn_ready")
                tr_ready = sem("tr_ready")
                xT_ready = sem("xT_ready")
                hi_ready = sem("hi_ready")
                lo_ready = sem("lo_ready")
                x_used = sem("x_used")
                out_ready = sem("out_ready")
                act_done = sem("act_done")
                u_done = sem("u_done")
                u_stored = [sem(f"u_stored{i}") for i in range(2)]
                g_stored = [sem(f"g_stored{i}") for i in range(2)]
                if conv:
                    taps = ConvTaps(name, stage, 3 if half == 0 else 0)
                block = stage.enter_context(nc.Block())
                if conv:
                    kinds = ["b", "a", "g"] * 4
                    w_at = [(4 if k == "b" else 0 if k == "a" else 8) + t // 3 for t, k in enumerate(kinds)]
                else:
                    kinds = ["u"] * 4 + ["g"] * 8
                    w_at = list(range(NT3))
                acts = [k != "a" for k in kinds]
                act_n = sum(acts)
                act_no = [sum(acts[:t]) for t in range(NT3)]
                HEAD, TAIL = (3, 1) if conv else (2, 2)

                def freed(eng, n, t, before):
                    if before * NT3 + t < BANKS3:
                        return
                    back, t0 = (0, t - BANKS3) if t >= BANKS3 else (1, t - BANKS3 + NT3)
                    if acts[t0]:
                        eng.wait_ge(act_done, (n - back) * act_n + act_no[t0] + 1)
                    else:
                        eng.wait_ge(u_done, (n - back) * 4 + t0 // 3 + 1)

                @block.sync
                def _(sp):
                    def load(n):
                        at_turn(sp, tr_ready, n * KT)
                        for s in range(TPC):
                            sp.dma_start(xin[:, s, :], x_rows[bass.ds(n * CW + s * P, P), :]).then_inc(x_loaded[s], 16)

                    def body(n, slot, before, after):
                        if before == 0 and not conv:
                            load_first_x(sp)
                        if after >= 1:
                            load(n + 1)
                        u_no = g_no = 0
                        cols = bass.ds(n * CW, CW)
                        for t in range(NT3):
                            if kinds[t] in "ua":
                                u_no += 1
                                if conv:
                                    at_turn(sp, u_done, n * 4 + u_no)
                                    dst = cuT_d[(4 * half + u_no - 1) * P:(4 * half + u_no) * P, bass.ds(n * CW + HALO, CW)]
                                else:
                                    at_turn(sp, act_done, n * act_n + act_no[t] + 1)
                                    dst = uT_d[(u_no - 1) * P:u_no * P, bass.ds(n * CW + PHALO, CW)]
                                i = (u_no - 1) % 2
                                sp.dma_start(dst, u_sb[:, i, :]).then_inc(u_stored[i], 16)
                            elif kinds[t] == "g":
                                g_no += 1
                                at_turn(sp, act_done, n * act_n + act_no[t] + 1)
                                if conv:
                                    dst = cgT_d[(4 * half + g_no - 1) * P:(4 * half + g_no) * P, cols]
                                else:
                                    dst = gT_d[(g_no - 1) * P:g_no * P, cols]
                                i = (g_no - 1) % 2
                                sp.dma_start(dst, g_sb[:, i, :]).then_inc(g_stored[i], 16)

                    chunks(sp, body, NCH, HEAD, TAIL)
                    for i in range(2):
                        sp.wait_ge(u_stored[i], 16 * NCH * 2)
                        sp.wait_ge(g_stored[i], 16 * NCH * (2 if conv else 4))

                @block.tensor
                def _(pe):
                    def transpose_x(n, k, before):
                        if k == 0:
                            pe.wait_ge(xn_ready, n + 1)
                        if before * KT + k >= 2:
                            pe.wait_ge(xT_ready, n * KT + k - 1)
                        for s in range(TPC):
                            ins = pe.transpose(tr_ps[:, k % 2, s * P:(s + 1) * P], xin[:, s, k * P:(k + 1) * P], ident[:])
                        ins.then_inc(tr_ready, 1)

                    def body(n, slot, before, after):
                        if before == 0:
                            for k in range(KT):
                                transpose_x(0, k, 0)
                        for t in range(NT3):
                            freed(pe, n, t, before)
                            cols = slice(w_at[t] * P, (w_at[t] + 1) * P)
                            for k in range(KT):
                                if t == 0:
                                    pe.wait_ge(lo_ready, n * KT + k + 1)
                                ins = product(pe, out_ps[:, t % BANKS3, :], (w_hi[:, k, cols], w_lo[:, k, cols]),
                                              (xT_hi[:, k, :], xT_lo[:, k, :]), k == 0, k == KT - 1)
                                if t == NT3 - 1:
                                    ins.then_inc(x_used, 1)
                                elif k == KT - 1:
                                    ins.then_inc(out_ready, 1)
                            if after >= 1 and 3 <= t < 3 + KT:
                                transpose_x(n + 1, t - 3, before + 1)

                    chunks(pe, body, NCH, HEAD, TAIL)

                def tile_ready(eng, n, t):
                    if t == NT3 - 1:
                        eng.wait_ge(x_used, (n + 1) * KT)
                    else:
                        eng.wait_ge(out_ready, n * (NT3 - 1) + t + 1)

                @block.scalar
                def _(act):
                    def scale_x(n):
                        for s in range(TPC):
                            act.wait_ge(x_loaded[s], 16 * (n + 1))
                            ins = act.activation(xin[:, s, :], xin[:, s, :], ACT.Copy, scale=rstd[:, bass.ds(n * TPC + s, 1)])
                        ins.then_inc(xn_ready, 1)

                    def evacuate_xT(n, k, before):
                        act.wait_ge(tr_ready, n * KT + k + 1)
                        if before >= 1:
                            act.wait_ge(lo_ready, (n - 1) * KT + k + 1)
                        act.activation(xT[:, k, :], tr_ps[:, k % 2, :], ACT.Identity,
                                       scale=G[:, which, k:k + 1], bias=S[:, which, k:k + 1]).then_inc(xT_ready, 1)

                    def split_hi(n, k, before):
                        act.wait_ge(xT_ready, n * KT + k + 1)
                        if before >= 1:
                            act.wait_ge(x_used, (n - 1) * KT + k + 1)
                        act.activation(xT_hi[:, k, :], xT[:, k, :], ACT.Copy).then_inc(hi_ready, 1)

                    def evacuate(n, t, before):
                        bank = out_ps[:, t % BANKS3, :]
                        tile_ready(act, n, t)
                        no = kinds[:t].count(kinds[t])
                        if kinds[t] == "b":
                            if before * 4 + no >= 2:
                                act.wait_ge(u_done, n * 4 + no - 1)
                            act.activation(sig[:, no % 2, :], bank, ACT.Sigmoid).then_inc(act_done, 1)
                        else:
                            per = kinds.count(kinds[t])
                            dst, stored = (u_sb, u_stored) if kinds[t] == "u" else (g_sb, g_stored)
                            if before * per + no >= 2:
                                act.wait_ge(stored[no % 2], 8 * (n * per + no - no % 2))
                            func = ACT.Silu if kinds[t] == "g" and not conv else ACT.Copy
                            act.activation(dst[:, no % 2, :], bank, func).then_inc(act_done, 1)

                    def body(n, slot, before, after):
                        if before == 0:
                            scale_x(0)
                            for k in range(KT):
                                evacuate_xT(0, k, 0)
                                split_hi(0, k, 0)
                        for t in range(NT3):
                            if t == 1 and after >= 1:
                                scale_x(n + 1)
                            if t == NT3 - 1 and after >= 1:
                                for k in range(KT):
                                    split_hi(n + 1, k, before + 1)
                            if acts[t]:
                                evacuate(n, t, before)
                            if after >= 1 and 3 <= t < 3 + KT:
                                evacuate_xT(n + 1, t - 3, before + 1)

                    chunks(act, body, NCH, HEAD, TAIL)

                @block.vector
                def _(dve):
                    def split_lo(n, k):
                        dve.wait_ge(hi_ready, n * KT + k + 1)
                        dve.tensor_tensor(xT_lo[:, k, :], xT[:, k, :], f32v(xT_hi[:, k, :]), ALU.subtract).then_inc(lo_ready, 1)

                    def gated(n, j, before):
                        dve.wait_ge(out_ready, n * (NT3 - 1) + 3 * j + 2)
                        dve.wait_ge(act_done, n * act_n + act_no[3 * j] + 1)
                        if before * 4 + j >= 2:
                            dve.wait_ge(u_stored[j % 2], 8 * (n * 4 + j - j % 2))
                        dve.tensor_tensor(u_sb[:, j % 2, :], out_ps[:, (3 * j + 1) % BANKS3, :], sig[:, j % 2, :], ALU.mult).then_inc(u_done, 1)

                    def body(n, slot, before, after):
                        if before == 0:
                            for k in range(KT):
                                split_lo(0, k)
                        if conv:
                            item = conv_order(half, before)
                            for j in range(4):
                                if item is not None:
                                    taps.run(dve, n, slot, before, item, j)
                                gated(n, j, before)
                        if after >= 1:
                            for k in range(KT):
                                split_lo(n + 1, k)

                    chunks(dve, body, NCH, HEAD, TAIL)

                @block.gpsimd
                def _(pool):
                    if not conv:
                        return
                    taps.give_credits(pool)

                    def load(n, slot, before):
                        item = conv_order(half, before)
                        if item is not None:
                            taps.load(pool, n, slot, item, u_stored if item[0] == half else None)

                    def body(n, slot, before, after):
                        if before == 0:
                            load(0, 0, 0)
                        if after >= 1:
                            load(n + 1, 1 - slot, before + 1)
                        item = conv_order(half, before)
                        if item is not None:
                            taps.store(pool, n, slot, item)

                    chunks(pool, body, NCH, HEAD, TAIL)
                    taps.finish(pool, NCH - (3 if half == 0 else 0))

        project("s3_", x[0], rstd0[:, CTX // P:], 0, ug_w, None)
        ug_keep.close()

        clear_semaphores()
        def load_out_weights(name, w_out, which, stage):
            w_hi = stage.enter_context(nc.sbuf_tensor(name + "w_hi", [P, KT, D], F32R))
            w_lo = stage.enter_context(nc.sbuf_tensor(name + "w_lo", [P, KT, D], F32R))
            with ExitStack() as inner:
                row = inner.enter_context(nc.sbuf_tensor(name + "gate", [P, D], F32))
                row_loaded = new_sem(inner, name + "gate_loaded")
                split_weights(name + "w", [(0, lambda k: w_out[0, k * P:(k + 1) * P, :], D)], w_hi, w_lo,
                              (row, row_loaded, gate_d[which:which + 1, :].partition_broadcast(P)))
            return w_hi, w_lo

        def out_product(pe, acc, y_hi, y_lo, w_hi, w_lo, s, k):
            ts = slice(s * P, (s + 1) * P)
            for h in range(2):
                cols = slice(512 * h, 512 * (h + 1))
                ins = product(pe, acc[:, h, :], (y_hi[:, k, ts], y_lo[:, k, ts]),
                              (w_hi[:, k, cols], w_lo[:, k, cols]), k == 0, k == KT - 1)
            return ins

        with ExitStack() as stage:
            sb = lambda n, s, d=F32: stage.enter_context(nc.sbuf_tensor("s4_" + n, s, d))
            ps = lambda n, s, d=F32: stage.enter_context(nc.psum_tensor("s4_" + n, s, d))
            sem = lambda n: new_sem(stage, "s4_" + n)
            NG = len(POOL_WINDOWS)
            UW = CW + 2 * PHALO
            w_hi, w_lo = load_out_weights("s4_", ap_w_out, 0, stage)
            pw_hi = sb("pw_hi", [P, NG, P], F32R)
            pw_lo = sb("pw_lo", [P, NG, P], F32R)
            split_weights("s4_pw", [(0, lambda k: ap_pool_w[0, k, :, :], P)], pw_hi, pw_lo)
            pscale = sb("pscale", [P, NG])
            a_in = sb("a_in", [P, NG, CW])
            y = sb("y", [P, 2, KT, CW])
            u_in = sb("u_in", [P, NG, UW])
            cnt = sb("cnt", [P, NG, CW])
            sums = sb("sums", [P, 2, UW])
            d = sb("d", [P, 2, CW])
            d_hi = sb("d_hi", [P, 2, CW], F32R)
            d_lo = sb("d_lo", [P, 2, CW], F32R)
            y_hi = sb("y_hi", [P, KT, CW], F32R)
            y_lo = sb("y_lo", [P, KT, CW], F32R)
            xr = sb("xr", [P, TPC, D])
            junk = sb("junk", [P, D])
            ss1 = sb("ss1", [P, TILES])
            tmp1 = sb("tmp1", [P, TILES])
            out_ps = ps("out_ps", [P, 2, 2, 512])
            pool_ps = ps("pool_ps", [P, NG, 512])
            pscale_loaded = sem("pscale_loaded")
            in_loaded = sem("in_loaded")
            g_loaded = [sem(f"g_loaded{i}") for i in range(2)]
            xr_loaded = [sem(f"xr_loaded{i}") for i in range(TPC)]
            sum_step = sem("sum_step")
            d_ready = sem("d_ready")
            d_hi_ready = sem("d_hi_ready")
            d_lo_ready = sem("d_lo_ready")
            pool_ready = sem("pool_ready")
            y_ready = sem("y_ready")
            hi_ready = sem("hi_ready")
            lo_ready = sem("lo_ready")
            y_used = sem("y_used")
            out_ready = sem("out_ready")
            x1_ready = sem("x1_ready")
            ss_ready = sem("ss_ready")
            x1_stored = [sem(f"x1_stored{i}") for i in range(TPC)]
            fin_step = sem("fin_step")
            block = stage.enter_context(nc.Block())
            HEAD, TAIL = 2, 2
            SUM_STEPS = sum(len(bin(w)) - 3 for w in POOL_WINDOWS) + NG

            @block.sync
            def _(sp):
                sp.dma_start(pscale[:], ap_pool_scale[0, :].rearrange("(g p) -> p g", p=P), allow_slow_non_contiguous=True).then_inc(pscale_loaded, 16)

                def load_in(n, slot, before):
                    cols = bass.ds(n * CW, CW)
                    if before >= 2:
                        at_turn(sp, lo_ready, (n - 1) * KT)
                    sp.dma_start(y[:, slot], gT_d[:, cols].rearrange("(k p) t -> p k t", p=P)).then_inc(g_loaded[slot], 16)
                    if before >= 1:
                        at_turn(sp, y_ready, n * KT)
                    sp.dma_start(a_in[:], aT_d[:, cols].rearrange("(k p) t -> p k t", p=P)).then_inc(in_loaded, 16)
                    sp.dma_start(u_in[:], uT_d[:, bass.ds(n * CW, UW)].rearrange("(k p) t -> p k t", p=P)).then_inc(in_loaded, 16)
                    sp.dma_start(cnt[:], counts[:, cols].partition_broadcast(P)).then_inc(in_loaded, 16)

                def load_x(n, s, before):
                    if before >= 1:
                        at_turn(sp, x1_stored[s], 16 * n)
                        at_turn(sp, ss_ready, (n - 1) * TPC + s + 1)
                    sp.dma_start(xr[:, s, :], x[0, bass.ds(n * CW + s * P, P), :]).then_inc(xr_loaded[s], 16)

                def body(n, slot, before, after):
                    if before == 0:
                        load_in(0, 0, 0)
                        for s in range(TPC):
                            load_x(0, s, 0)
                        load_in(1, 1, 1)
                    for s in range(TPC):
                        at_turn(sp, x1_ready, n * TPC + s + 1)
                        sp.dma_start(x1_d[bass.ds(n * CW + s * P, P), :], xr[:, s, :]).then_inc(x1_stored[s], 16)
                        if after >= 2 and s == 1:
                            load_in(n + 2, slot, before + 2)
                        if after >= 1 and s >= 2:
                            load_x(n + 1, s - 2, before + 1)
                    if after >= 1:
                        for s in (2, 3):
                            load_x(n + 1, s, before + 1)

                chunks(sp, body, NCH, HEAD, TAIL)
                for s in range(TPC):
                    sp.wait_ge(x1_stored[s], 16 * NCH)

            @block.tensor
            def _(pe):
                def pool_product(n, g, before):
                    pe.wait_ge(d_lo_ready, n * NG + g + 1)
                    if before >= 1:
                        pe.wait_ge(y_ready, (n - 1) * KT + NG + g + 1)
                    product(pe, pool_ps[:, g, :], (pw_hi[:, g, :], pw_lo[:, g, :]),
                            (d_hi[:, g % 2, :], d_lo[:, g % 2, :]), True, True).then_inc(pool_ready, 1)

                def body(n, slot, before, after):
                    if before == 0:
                        for g in range(NG):
                            pool_product(0, g, 0)
                    for s in range(TPC):
                        if before * TPC + s >= 2:
                            pe.wait_ge(x1_ready, n * TPC + s - 1)
                        for k in range(KT):
                            if s == 0:
                                pe.wait_ge(lo_ready, n * KT + k + 1)
                            ins = out_product(pe, out_ps[:, s % 2], y_hi, y_lo, w_hi, w_lo, s, k)
                            if s == TPC - 1:
                                ins.then_inc(y_used, 1)
                            elif k == KT - 1:
                                ins.then_inc(out_ready, 1)
                        if after >= 1 and s < 2:
                            for g in (2 * s, 2 * s + 1):
                                pool_product(n + 1, g, before + 1)

                chunks(pe, body, NCH, HEAD, TAIL)

            @block.scalar
            def _(act):
                def split_d(n, g, before):
                    act.wait_ge(d_ready, n * NG + g + 1)
                    if before * NG + g >= 2:
                        act.wait_ge(pool_ready, n * NG + g - 1)
                    act.activation(d_hi[:, g % 2, :], d[:, g % 2, :], ACT.Copy).then_inc(d_hi_ready, 1)

                def split_y(n, slot, k, before):
                    act.wait_ge(y_ready, n * KT + k + 1)
                    if before >= 1:
                        act.wait_ge(y_used, (n - 1) * KT + k + 1)
                    act.activation(y_hi[:, k, :], y[:, slot, k, :], ACT.Copy).then_inc(hi_ready, 1)

                def squares(n, s, before):
                    act.wait_ge(x1_ready, n * TPC + s + 1)
                    if before * TPC + s >= 1:
                        act.wait_ge(ss_ready, n * TPC + s)
                    act.activation(junk[:], xr[:, s, :], ACT.Square, accum_out=ss1[:, bass.ds(n * TPC + s, 1)]).then_inc(ss_ready, 1)

                def body(n, slot, before, after):
                    if before == 0:
                        for g in range(NG):
                            split_d(0, g, 0)
                        for k in range(KT):
                            split_y(0, 0, k, 0)
                    for s in range(TPC):
                        if after >= 1 and s < 2:
                            split_d(n + 1, 2 * s, before + 1)
                            split_d(n + 1, 2 * s + 1, before + 1)
                        if after >= 1 and s == TPC - 1:
                            for k in range(KT):
                                split_y(n + 1, 1 - slot, k, before + 1)
                        squares(n, s, before)

                chunks(act, body, NCH, HEAD, TAIL)

            @block.vector
            def _(dve):
                def gate_attention(n, slot, k):
                    if k == 0:
                        dve.wait_ge(g_loaded[slot], 8 * (n + 2 - slot))
                    dve.tensor_tensor(y[:, slot, k, :], y[:, slot, k, :], a_in[:, k, :], ALU.mult).then_inc(y_ready, 1)

                def pool_mean(n, g, before):
                    step = n * SUM_STEPS + sum(len(bin(w)) - 3 for w in POOL_WINDOWS[:g]) + g
                    w = POOL_WINDOWS[g]
                    at = PHALO - w // 2
                    if g == 0:
                        dve.wait_ge(in_loaded, 48 * (n + 1))
                    if before * NG + g >= 1:
                        dve.wait_ge(d_ready, n * NG + g)
                    src, width = u_in[:, g, :], 1
                    while width < w:
                        length = CW + w - 2 * width
                        dst = sums[:, (width.bit_length() - 1) % 2, :]
                        dve.tensor_tensor(dst[:, at:at + length], src[:, at:at + length], src[:, at + width:at + width + length], ALU.add).then_inc(sum_step, 1)
                        step = step + 1
                        dve.wait_ge(sum_step, step)
                        src, width = dst, 2 * width
                    dve.tensor_tensor(src[:, at:at + CW], src[:, at:at + CW], cnt[:, g, :], ALU.mult).then_inc(sum_step, 1)
                    dve.wait_ge(sum_step, step + 1)
                    if before * NG + g >= 2:
                        dve.wait_ge(d_lo_ready, n * NG + g - 1)
                    dve.tensor_tensor(d[:, g % 2, :], src[:, at:at + CW], u_in[:, g, PHALO:PHALO + CW], ALU.subtract).then_inc(d_ready, 1)

                def split_d(n, g, before):
                    dve.wait_ge(d_hi_ready, n * NG + g + 1)
                    if before * NG + g >= 2:
                        dve.wait_ge(pool_ready, n * NG + g - 1)
                    dve.tensor_tensor(d_lo[:, g % 2, :], d[:, g % 2, :], f32v(d_hi[:, g % 2, :]), ALU.subtract).then_inc(d_lo_ready, 1)

                def gate_pool(n, slot, g):
                    dve.wait_ge(pool_ready, n * NG + g + 1)
                    dve.scalar_tensor_tensor(y[:, slot, NG + g, :], pool_ps[:, g, :], pscale[:, g:g + 1], y[:, slot, NG + g, :],
                                             ALU.mult, ALU.mult).then_inc(y_ready, 1)

                def split_y(n, slot, k):
                    dve.wait_ge(hi_ready, n * KT + k + 1)
                    dve.tensor_tensor(y_lo[:, k, :], y[:, slot, k, :], f32v(y_hi[:, k, :]), ALU.subtract).then_inc(lo_ready, 1)

                def residual(n, s):
                    if s == TPC - 1:
                        dve.wait_ge(y_used, (n + 1) * KT)
                    else:
                        dve.wait_ge(out_ready, n * (TPC - 1) + s + 1)
                    dve.wait_ge(xr_loaded[s], 16 * (n + 1))
                    dve.tensor_tensor(xr[:, s, :], xr[:, s, :], out_ps[:, s % 2].rearrange("p h c -> p (h c)"), ALU.add).then_inc(x1_ready, 1)

                dve.wait_ge(pscale_loaded, 16)

                def prepare(n, slot, before, part):
                    if part == 0:
                        for g in range(NG):
                            pool_mean(n, g, before)
                            gate_attention(n, slot, g)
                            split_d(n, g, before)
                    elif part == 1:
                        for g in range(NG):
                            gate_pool(n, slot, g)
                    else:
                        for k in range(KT):
                            split_y(n, slot, k)

                def body(n, slot, before, after):
                    if before == 0:
                        for part in range(3):
                            prepare(0, 0, 0, part)
                    if after >= 1:
                        pool_mean(n + 1, 0, before + 1)
                        gate_attention(n + 1, 1 - slot, 0)
                        split_d(n + 1, 0, before + 1)
                        pool_mean(n + 1, 1, before + 1)
                        gate_attention(n + 1, 1 - slot, 1)
                        split_d(n + 1, 1, before + 1)
                    residual(n, 0)
                    if after >= 1:
                        pool_mean(n + 1, 2, before + 1)
                        gate_attention(n + 1, 1 - slot, 2)
                        split_d(n + 1, 2, before + 1)
                        pool_mean(n + 1, 3, before + 1)
                        gate_attention(n + 1, 1 - slot, 3)
                        split_d(n + 1, 3, before + 1)
                    residual(n, 1)
                    if after >= 1:
                        prepare(n + 1, 1 - slot, before + 1, 1)
                    residual(n, 2)
                    if after >= 1:
                        prepare(n + 1, 1 - slot, before + 1, 2)
                    residual(n, 3)

                chunks(dve, body, NCH, HEAD, TAIL)
                dve.wait_ge(ss_ready, TILES)
                dve.tensor_scalar(ss1[:], ss1[:], 1.0 / D, EPS, ALU.mult, ALU.add).then_inc(fin_step, 1)
                dve.wait_ge(fin_step, 1)
                rsqrt(dve, fin_step, 1, rstd1[:], ss1[:], tmp1[:])

        clear_semaphores()
        for half in range(2):
            if half == 1:
                clear_semaphores()
            cols = lambda k, part, half=half: cv_w_in[0, k * P:(k + 1) * P, part * D + half * 512:part * D + half * 512 + 512]
            project(f"s5{'ab'[half]}_", x1_d, rstd1[:, :], 2,
                    [(512 * part, lambda k, part=part: cols(k, part), 512) for part in range(3)], half)

        clear_semaphores()
        w6_hi = whole.enter_context(nc.sbuf_tensor("s6_w_hi", [P, KT, D], F32R))
        w6_lo = whole.enter_context(nc.sbuf_tensor("s6_w_lo", [P, KT, D], F32R))
        with ExitStack() as stage:
            sb = lambda n, s, d=F32: stage.enter_context(nc.sbuf_tensor("s5c_" + n, s, d))
            sem = lambda n: new_sem(stage, "s5c_" + n)
            items = [((2, 3), 2), ((0, 1), 3), ((2, 3), 3)]
            PE_TAPS = 15
            DVE_TAPS = CONV_K - PE_TAPS
            UC = PAIR + 2 * HALO
            raw = sb("raw", [P, 2, D])
            row = sb("gate", [P, D])
            cw_hi = sb("cw_hi", [P, KT, CONV_K], F32R)
            cw_lo = sb("cw_lo", [P, KT, CONV_K], F32R)
            u = sb("u", [P, 2, 2, UC])
            u_hi = sb("u_hi", [P, 2, 2, UC], F32R)
            u_lo = sb("u_lo", [P, 2, 2, UC], F32R)
            acc = sb("acc", [P, 2, 2, PAIR])
            diag = sb("diag", [P, 4, PE_TAPS, 2, P], F32R)
            conv_ps = stage.enter_context(nc.psum_tensor("s5c_conv_ps", [P, 2, 2, PAIR], F32))
            u_loaded = [sem(f"u_loaded{i}") for i in range(2)]
            row_loaded = sem("row_loaded")
            raw_loaded = [sem(f"raw_loaded{i}") for i in range(2)]
            folded = sem("folded")
            w_hi_ready = sem("w_hi_ready")
            w_split = sem("w_split")
            cw_split = sem("cw_split")
            u_hi_ready = sem("u_hi_ready")
            u_lo_ready = sem("u_lo_ready")
            diag_ready = sem("diag_ready")
            ps_ready = sem("ps_ready")
            step = sem("step")
            stored = [sem(f"stored{i}") for i in range(2)]
            block = stage.enter_context(nc.Block())
            ITEM_STEPS = 2 * (DVE_TAPS + 1)
            diag_order = (2, 3, 0, 1)
            rows = lambda t: slice((4 + t) * P, (5 + t) * P)

            @block.sync
            def _(sp):
                def load_u(o):
                    tiles, pair = items[o]
                    if o >= 2:
                        sp.wait_ge(step, (o - 1) * ITEM_STEPS)
                    for i, t in enumerate(tiles):
                        sp.dma_start(u[:, o % 2, i, :], cuT_d[rows(t), pair * PAIR:pair * PAIR + UC]).then_inc(u_loaded[o % 2], 16)

                def load_w(k):
                    if k >= 2:
                        sp.wait_ge(w_split, k - 1)
                    sp.dma_start(raw[:, k % 2, :], cv_w_out[0, k * P:(k + 1) * P, :]).then_inc(raw_loaded[k % 2], 16)

                load_u(0)
                load_u(1)
                sp.dma_start(row[:], gate_d[1:2, :].partition_broadcast(P)).then_inc(row_loaded, 16)
                for k in range(KT):
                    load_w(k)
                for o, (tiles, pair) in enumerate(items):
                    if o == 1:
                        load_u(2)
                    sp.wait_ge(step, (o + 1) * ITEM_STEPS)
                    for i, t in enumerate(tiles):
                        sp.dma_start(ccT_d[rows(t), pair * PAIR:(pair + 1) * PAIR], acc[:, o % 2, i, :]).then_inc(stored[o % 2], 16)
                for i in range(2):
                    sp.wait_ge(stored[i], 32 * len(items[i::2]))

            @block.gpsimd
            def _(pool):
                pool.wait_ge(row_loaded, 16)
                for k in range(KT):
                    pool.wait_ge(raw_loaded[k % 2], 16 * (k // 2 + 1))
                    pool.tensor_tensor(raw[:, k % 2, :], raw[:, k % 2, :], row[:], ALU.mult).then_inc(folded, 1)
                    pool.wait_ge(w_hi_ready, k + 1)
                    pool.tensor_tensor(w6_lo[:, k, :], raw[:, k % 2, :], f32v(w6_hi[:, k, :]), ALU.subtract).then_inc(w_split, 1)

            @block.scalar
            def _(act):
                def split_u(o):
                    act.wait_ge(u_loaded[o % 2], 32 * (o // 2 + 1))
                    if o >= 2:
                        act.wait_ge(ps_ready, 2 * (o - 1))
                    for i in range(2):
                        act.activation(u_hi[:, o % 2, i, :], u[:, o % 2, i, :], ACT.Copy).then_inc(u_hi_ready, 1)

                def diagonals(t):
                    for x in range(PE_TAPS):
                        for part, w in enumerate((cw_hi, cw_lo)):
                            ins = act.activation(diag[:, t, x, part, :], ident[:], ACT.Copy,
                                                 scale=f32v(w[:, 4 + t, DVE_TAPS + x:DVE_TAPS + x + 1]))
                    ins.then_inc(diag_ready, 1)

                split_u(0)
                act.wait_ge(cw_split, 2)
                for t in diag_order[0:2]:
                    diagonals(t)
                split_u(1)
                for t in diag_order[2:4]:
                    diagonals(t)
                for k in range(KT):
                    act.wait_ge(folded, k + 1)
                    act.activation(w6_hi[:, k, :], raw[:, k % 2, :], ACT.Copy).then_inc(w_hi_ready, 1)
                split_u(2)

            @block.tensor
            def _(pe):
                for o, (tiles, pair) in enumerate(items):
                    if o >= 2:
                        pe.wait_ge(step, (o - 1) * ITEM_STEPS)
                    for i, t in enumerate(tiles):
                        pe.wait_ge(diag_ready, diag_order.index(t) + 1)
                        pe.wait_ge(u_lo_ready, 2 * o + i + 1)
                        for h in range(2):
                            for x in range(PE_TAPS):
                                at = h * CW + DVE_TAPS + x
                                ins = product(pe, conv_ps[:, o % 2, i, h * CW:(h + 1) * CW], (diag[:, t, x, 0, :], diag[:, t, x, 1, :]),
                                              (u_hi[:, o % 2, i, at:at + CW], u_lo[:, o % 2, i, at:at + CW]), x == 0, x == PE_TAPS - 1)
                        ins.then_inc(ps_ready, 1)

            @block.vector
            def _(dve):
                dve.tensor_copy(cw_hi[:, 4:KT], conv_w[:, 4:KT]).then_inc(cw_split, 1)
                dve.wait_ge(cw_split, 1)
                dve.tensor_tensor(cw_lo[:, 4:KT], conv_w[:, 4:KT], f32v(cw_hi[:, 4:KT]), ALU.subtract).then_inc(cw_split, 1)
                for o, (tiles, pair) in enumerate(items):
                    for i in range(2):
                        dve.wait_ge(u_hi_ready, 2 * o + i + 1)
                        dve.tensor_tensor(u_lo[:, o % 2, i, :], u[:, o % 2, i, :], f32v(u_hi[:, o % 2, i, :]), ALU.subtract).then_inc(u_lo_ready, 1)
                    if o >= 2:
                        dve.wait_ge(stored[o % 2], 32)
                    for tap in range(DVE_TAPS):
                        for i, t in enumerate(tiles):
                            w = conv_w[:, 4 + t, tap:tap + 1]
                            src = u[:, o % 2, i, tap:tap + PAIR]
                            dst = acc[:, o % 2, i, :]
                            if tap == 0:
                                dve.tensor_scalar(dst, src, w, conv_b[:, 4 + t:5 + t], ALU.mult, ALU.add).then_inc(step, 1)
                            else:
                                dve.wait_ge(step, o * ITEM_STEPS + 2 * tap + i - 1)
                                dve.scalar_tensor_tensor(dst, src, w, dst, ALU.mult, ALU.add).then_inc(step, 1)
                    for i in range(2):
                        dve.wait_ge(ps_ready, 2 * o + i + 1)
                        dve.wait_ge(step, o * ITEM_STEPS + 2 * DVE_TAPS + i - 1)
                        dve.tensor_tensor(acc[:, o % 2, i, :], acc[:, o % 2, i, :], conv_ps[:, o % 2, i, :], ALU.add).then_inc(step, 1)

        clear_semaphores()
        with ExitStack() as stage:
            sb = lambda n, s, d=F32: stage.enter_context(nc.sbuf_tensor("s6_" + n, s, d))
            ps = lambda n, s, d=F32: stage.enter_context(nc.psum_tensor("s6_" + n, s, d))
            sem = lambda n: new_sem(stage, "s6_" + n)
            w_hi, w_lo = w6_hi, w6_lo
            averager = sb("averager", [P, P])
            ln_g = sb("ln_g", [P, KT])
            ln_b = sb("ln_b", [P, KT])
            norm_g = sb("norm_g", [P, D])
            z = sb("z", [P, 2, KT, CW])
            y = sb("y", [P, KT, CW])
            ch_sum = sb("ch_sum", [P, CW])
            sq = sb("sq", [P, 4, CW])
            sq_sum = sb("sq_sum", [P, CW])
            ln_var = sb("ln_var", [P, CW])
            ln_rstd = sb("ln_rstd", [P, CW])
            ln_tmp = sb("ln_tmp", [P, CW])
            y_hi = sb("y_hi", [P, KT, CW], F32R)
            y_lo = sb("y_lo", [P, KT, CW], F32R)
            xr = sb("xr", [P, 2, TPC, D])
            junk = sb("junk", [P, D])
            ss = sb("ss", [P, TPC])
            fin_var = sb("fin_var", [P, TPC])
            fin_rstd = sb("fin_rstd", [P, TPC])
            fin_tmp = sb("fin_tmp", [P, TPC])
            out_ps = ps("out_ps", [P, 2, 2, 512])
            mean_ps = ps("mean_ps", [P, CW])
            var_ps = ps("var_ps", [P, CW])
            fixed_loaded = sem("fixed_loaded")
            averager_made = sem("averager_made")
            z_loaded = [sem(f"z_loaded{i}") for i in range(2)]
            g_loaded = sem("g_loaded")
            xr_loaded = [sem(f"xr_loaded{i}") for i in range(2)]
            sum_step = sem("sum_step")
            mean_ready = sem("mean_ready")
            centred = sem("centred")
            sq_ready = sem("sq_ready")
            sq_step = sem("sq_step")
            var_ready = sem("var_ready")
            rs_step = sem("rs_step")
            z_ready = sem("z_ready")
            sg_ready = sem("sg_ready")
            ln_ready = sem("ln_ready")
            y_ready = sem("y_ready")
            hi_ready = sem("hi_ready")
            lo_ready = sem("lo_ready")
            y_used = sem("y_used")
            out_ready = sem("out_ready")
            x2_ready = sem("x2_ready")
            ss_ready = sem("ss_ready")
            fin_step = sem("fin_step")
            fin_scaled = sem("fin_scaled")
            o_ready = sem("o_ready")
            o_stored = [sem(f"o_stored{i}") for i in range(2)]
            block = stage.enter_context(nc.Block())
            HEAD, TAIL = 2, 2
            SUMS = KT - 1

            @block.sync
            def _(sp):
                def load_z(n, slot, before):
                    if before >= 2:
                        at_turn(sp, y_ready, (n - 1) * KT)
                    sp.dma_start(z[:, slot], ccT_d[:, bass.ds(n * CW, CW)].rearrange("(k p) t -> p k t", p=P)).then_inc(z_loaded[slot], 16)

                def load_g(n, before):
                    if before >= 1:
                        at_turn(sp, lo_ready, n * KT)
                    sp.dma_start(y[:], cgT_d[:, bass.ds(n * CW, CW)].rearrange("(k p) t -> p k t", p=P)).then_inc(g_loaded, 16)

                def load_x(n, slot, before, s):
                    if before >= 2:
                        at_turn(sp, o_stored[slot], 8 * TPC * (n - slot))
                    sp.dma_start(xr[:, slot, s, :], x1_d[bass.ds(n * CW + s * P, P), :]).then_inc(xr_loaded[slot], 16)

                def store(n, slot):
                    for s in range(TPC):
                        at_turn(sp, o_ready, n * TPC + s + 1)
                        sp.dma_start(out[0, bass.ds(n * CW + s * P, P), :], xr[:, slot, s, :]).then_inc(o_stored[slot], 16)

                def body(n, slot, before, after):
                    if before == 0:
                        load_z(0, 0, 0)
                        load_g(0, 0)
                        load_z(1, 1, 1)
                        for s in range(TPC):
                            load_x(0, 0, 0, s)
                    if after >= 2:
                        load_z(n + 2, slot, before + 2)
                    if after >= 1:
                        load_g(n + 1, before + 1)
                    if before >= 1:
                        store(n - 1, 1 - slot)
                    if after >= 1:
                        for s in range(TPC):
                            load_x(n + 1, 1 - slot, before + 1, s)

                smalls = [(ln_g[:], cv_ln_g[0, :].rearrange("(k p) -> p k", p=P)), (ln_b[:], cv_ln_b[0, :].rearrange("(k p) -> p k", p=P)),
                          (norm_g[:], final_norm_g.rearrange("(a d) -> a d", a=1).partition_broadcast(P))]
                for dst, src in smalls:
                    sp.dma_start(dst, src, allow_slow_non_contiguous=True).then_inc(fixed_loaded, 16)
                chunks(sp, body, NCH, HEAD, TAIL)
                store(NCH - 1, (NCH - 1) % 2)
                for slot in range(2):
                    sp.wait_ge(o_stored[slot], 16 * TPC * NCH // 2)

            @block.gpsimd
            def _(pool):
                pool.memset(averager[:], 1.0 / D).then_inc(averager_made, 1)
                pool.wait_ge(fixed_loaded, 48)

                def channel_sums(n, slot, before):
                    pool.wait_ge(z_loaded[slot], 8 * (n + 2 - slot))
                    if before >= 1:
                        pool.wait_ge(mean_ready, n)
                    for k in range(1, KT):
                        if k == 1:
                            ins = pool.tensor_tensor(ch_sum[:], z[:, slot, 0, :], z[:, slot, 1, :], ALU.add)
                        else:
                            pool.wait_ge(sum_step, n * SUMS + k - 1)
                            ins = pool.tensor_tensor(ch_sum[:], ch_sum[:], z[:, slot, k, :], ALU.add)
                        ins.then_inc(sum_step, 1)

                def weigh(n, slot):
                    for s in range(TPC):
                        pool.wait_ge(fin_scaled, n * TPC + s + 1)
                        pool.tensor_tensor(xr[:, slot, s, :], xr[:, slot, s, :], norm_g[:], ALU.mult).then_inc(o_ready, 1)

                def body(n, slot, before, after):
                    if before == 0:
                        channel_sums(0, 0, 0)
                        channel_sums(1, 1, 1)
                    if after >= 2:
                        channel_sums(n + 2, slot, before + 2)
                    if before >= 1:
                        weigh(n - 1, 1 - slot)

                chunks(pool, body, NCH, HEAD, TAIL)
                weigh(NCH - 1, (NCH - 1) % 2)

            @block.tensor
            def _(pe):
                def mean(n, before):
                    pe.wait_ge(sum_step, (n + 1) * SUMS)
                    if before >= 1:
                        pe.wait_ge(centred, n * KT)
                    pe.matmul(mean_ps[:], averager[:], ch_sum[:], start=True, stop=True).then_inc(mean_ready, 1)

                def variance(n, before):
                    pe.wait_ge(sq_step, (n + 1) * SUMS)
                    if before >= 1:
                        pe.wait_ge(rs_step, (n - 1) * (RSQRT_STEPS + 1) + 1)
                    pe.matmul(var_ps[:], averager[:], sq_sum[:], start=True, stop=True).then_inc(var_ready, 1)

                pe.wait_ge(averager_made, 1)

                def body(n, slot, before, after):
                    if before == 0:
                        mean(0, 0)
                        variance(0, 0)
                        mean(1, 1)
                    for s in range(TPC):
                        if before * TPC + s >= 2:
                            pe.wait_ge(x2_ready, n * TPC + s - 1)
                        if after >= 2 and s == 1:
                            mean(n + 2, before + 2)
                        for k in range(KT):
                            if s == 0:
                                pe.wait_ge(lo_ready, n * KT + k + 1)
                            ins = out_product(pe, out_ps[:, s % 2], y_hi, y_lo, w_hi, w_lo, s, k)
                            if s == TPC - 1:
                                ins.then_inc(y_used, 1)
                            elif k == KT - 1:
                                ins.then_inc(out_ready, 1)
                            if before == 0 and s == 1 and k == 0:
                                variance(1, 1)
                            if after >= 2 and s == TPC - 1 and k == KT - 2:
                                variance(n + 2, before + 2)

                chunks(pe, body, NCH, HEAD, TAIL)

            @block.scalar
            def _(act):
                def square(n, slot, k, before):
                    act.wait_ge(centred, n * KT + k + 1)
                    if before * KT + k >= 4:
                        act.wait_ge(sq_step, n * SUMS + (max(k - 4, 1) if k >= 4 else 0))
                    act.activation(sq[:, k % 4, :], z[:, slot, k, :], ACT.Square).then_inc(sq_ready, 1)

                def silu_gate(n, k):
                    if k == 0:
                        act.wait_ge(g_loaded, 16 * (n + 1))
                    act.activation(y[:, k, :], y[:, k, :], ACT.Silu).then_inc(sg_ready, 1)

                def silu_ln(n, slot, k):
                    act.wait_ge(z_ready, n * KT + k + 1)
                    act.activation(z[:, slot, k, :], z[:, slot, k, :], ACT.Silu, scale=ln_g[:, k:k + 1],
                                   bias=ln_b[:, k:k + 1]).then_inc(ln_ready, 1)

                def split_hi(n, k, before):
                    act.wait_ge(y_ready, n * KT + k + 1)
                    if before >= 1:
                        act.wait_ge(y_used, (n - 1) * KT + k + 1)
                    act.activation(y_hi[:, k, :], y[:, k, :], ACT.Copy).then_inc(hi_ready, 1)

                def squares(n, slot, s, before):
                    act.wait_ge(x2_ready, n * TPC + s + 1)
                    if before * TPC + s >= 1:
                        act.wait_ge(ss_ready, n * TPC + s)
                    if before >= 1 and s == 0:
                        act.wait_ge(fin_step, (n - 1) * (RSQRT_STEPS + 1) + 1)
                    act.activation(junk[:], xr[:, slot, s, :], ACT.Square, accum_out=ss[:, s:s + 1]).then_inc(ss_ready, 1)

                def scale_out(n, slot):
                    act.wait_ge(fin_step, (n + 1) * (RSQRT_STEPS + 1))
                    for s in range(TPC):
                        act.activation(xr[:, slot, s, :], xr[:, slot, s, :], ACT.Copy, scale=fin_rstd[:, s:s + 1]).then_inc(fin_scaled, 1)

                act.wait_ge(fixed_loaded, 48)

                def body(n, slot, before, after):
                    if before == 0:
                        for k in range(KT):
                            square(0, 0, k, 0)
                        for k in range(KT):
                            silu_gate(0, k)
                            silu_ln(0, 0, k)
                        for k in range(KT):
                            split_hi(0, k, 0)
                        for k in range(KT):
                            square(1, 1, k, 1)
                    if after >= 1:
                        for k in range(KT):
                            silu_gate(n + 1, k)
                    squares(n, slot, 0, before)
                    if after >= 1:
                        for k in range(KT):
                            silu_ln(n + 1, 1 - slot, k)
                    if before >= 1:
                        scale_out(n - 1, 1 - slot)
                    for k in range(KT):
                        if after >= 2:
                            square(n + 2, slot, k, before + 2)
                        if k == KT // 2 - 1:
                            squares(n, slot, 1, before)
                    squares(n, slot, 2, before)
                    if after >= 1:
                        for k in range(KT):
                            split_hi(n + 1, k, before + 1)
                    squares(n, slot, 3, before)

                chunks(act, body, NCH, HEAD, TAIL)
                scale_out(NCH - 1, (NCH - 1) % 2)

            @block.vector
            def _(dve):
                def centre(n, slot, k):
                    if k == 0:
                        dve.wait_ge(mean_ready, n + 1)
                    dve.tensor_tensor(z[:, slot, k, :], z[:, slot, k, :], mean_ps[:], ALU.subtract).then_inc(centred, 1)

                def add_square(n, k, before):
                    if k == 0:
                        return
                    dve.wait_ge(sq_ready, n * KT + k + 1)
                    if k == 1:
                        if before >= 1:
                            dve.wait_ge(var_ready, n)
                        ins = dve.tensor_tensor(sq_sum[:], sq[:, 0, :], sq[:, 1, :], ALU.add)
                    else:
                        dve.wait_ge(sq_step, n * SUMS + k - 1)
                        ins = dve.tensor_tensor(sq_sum[:], sq_sum[:], sq[:, k % 4, :], ALU.add)
                    ins.then_inc(sq_step, 1)

                def normalise(n, slot, before):
                    dve.wait_ge(var_ready, n + 1)
                    if before >= 1:
                        dve.wait_ge(z_ready, n * KT)
                    dve.tensor_scalar(ln_var[:], var_ps[:], EPS, None, ALU.add).then_inc(rs_step, 1)
                    step = n * (RSQRT_STEPS + 1) + 1
                    dve.wait_ge(rs_step, step)
                    rsqrt(dve, rs_step, step, ln_rstd[:], ln_var[:], ln_tmp[:])

                def scale(n, slot, k):
                    dve.wait_ge(sq_ready, n * KT + k + 1)
                    dve.tensor_tensor(z[:, slot, k, :], z[:, slot, k, :], ln_rstd[:], ALU.mult).then_inc(z_ready, 1)

                def gate_y(n, slot, k):
                    dve.wait_ge(sg_ready, n * KT + k + 1)
                    dve.wait_ge(ln_ready, n * KT + k + 1)
                    dve.tensor_tensor(y[:, k, :], y[:, k, :], z[:, slot, k, :], ALU.mult).then_inc(y_ready, 1)

                def split_y(n, k):
                    dve.wait_ge(hi_ready, n * KT + k + 1)
                    dve.tensor_tensor(y_lo[:, k, :], y[:, k, :], f32v(y_hi[:, k, :]), ALU.subtract).then_inc(lo_ready, 1)

                def residual(n, slot, s):
                    if s == TPC - 1:
                        dve.wait_ge(y_used, (n + 1) * KT)
                    else:
                        dve.wait_ge(out_ready, n * (TPC - 1) + s + 1)
                    if s == 0:
                        dve.wait_ge(xr_loaded[slot], 8 * TPC * (n + 2 - slot))
                    dve.tensor_tensor(xr[:, slot, s, :], xr[:, slot, s, :], out_ps[:, s % 2].rearrange("p h c -> p (h c)"), ALU.add).then_inc(x2_ready, 1)

                def final_norm(n, before):
                    dve.wait_ge(ss_ready, (n + 1) * TPC)
                    if before >= 1:
                        dve.wait_ge(fin_scaled, n * TPC)
                    dve.tensor_scalar(fin_var[:], ss[:], 1.0 / D, EPS, ALU.mult, ALU.add).then_inc(fin_step, 1)
                    step = n * (RSQRT_STEPS + 1) + 1
                    dve.wait_ge(fin_step, step)
                    rsqrt(dve, fin_step, step, fin_rstd[:], fin_var[:], fin_tmp[:])

                def body(n, slot, before, after):
                    if before == 0:
                        for m in range(2):
                            for k in range(KT):
                                centre(m, m, k)
                                if k >= 1:
                                    add_square(m, k - 1, m)
                            add_square(m, KT - 1, m)
                            if m == 0:
                                normalise(0, 0, 0)
                                for k in range(KT):
                                    scale(0, 0, k)
                                for k in range(KT):
                                    gate_y(0, 0, k)
                                for k in range(KT):
                                    split_y(0, k)
                    if after >= 1:
                        normalise(n + 1, 1 - slot, before + 1)
                    residual(n, slot, 0)
                    if before >= 1:
                        final_norm(n - 1, before - 1)
                    if after >= 1:
                        for k in range(KT):
                            scale(n + 1, 1 - slot, k)
                    if after >= 2:
                        for k in range(KT):
                            centre(n + 2, slot, k)
                    residual(n, slot, 1)
                    for k in range(KT):
                        if after >= 1:
                            gate_y(n + 1, 1 - slot, k)
                        if after >= 2:
                            add_square(n + 2, k, before + 2)
                    residual(n, slot, 2)
                    if after >= 1:
                        for k in range(KT):
                            split_y(n + 1, k)
                    residual(n, slot, 3)

                chunks(dve, body, NCH, HEAD, TAIL)
                final_norm(NCH - 1, 9)


def kernel(**inputs):
    import concourse.bacc as bacc
    from concourse.bass_utils import run_bass_kernel_spmd

    nc = bacc.Bacc("TRN2", target_bir_lowering=False, num_devices=1)
    names = ["x", "c", "ctx", "c_ctx", "ap_ada_w", "ap_ada_b", "ap_norm_g", "ap_w_in", "ap_w_out", "ap_sink",
             "ap_pool_w", "ap_pool_scale", "cv_ada_w", "cv_ada_b", "cv_norm_g", "cv_w_in", "cv_w_out", "cv_dw_w",
             "cv_dw_b", "cv_ln_g", "cv_ln_b", "final_norm_g"]
    arrays = {"in_" + n: np.ascontiguousarray(inputs[n]) for n in names}
    arrays["rope"] = rope_tables()
    arrays["counts"] = pool_counts()
    arrays["masks"] = band_masks()
    aps = [nc.dram_tensor(n, a.shape, mybir.dt.from_np(a.dtype), kind="ExternalInput").ap() for n, a in arrays.items()]
    out = nc.dram_tensor("out", (1, SEQ, D), F32, kind="ExternalOutput").ap()
    build(nc, *aps, out)
    r = run_bass_kernel_spmd(nc, [arrays], core_ids=[0])
    return r.results[0]["out"]
```
